# Optimizing a Trainium2 kernel written in Bass

```python
import math
import jax, jax.numpy as jnp
from jax import lax
import numpy as np

D_MODEL = 1024
BATCH = 1
SEQ = 256
DEPTH = 2

CHUNK = 64
Q_BLOCK = 128
N_MIXERS = 2
N_RET_LAYERS = (DEPTH + 1) // 2
N_DIFF_LAYERS = DEPTH // 2
MIX_WIDTH = D_MODEL
MEM_LEN = 256
MEM_HEADS = 4
MEM_HEAD_DIM = 64
MEM_WIDTH = MEM_HEADS * MEM_HEAD_DIM
MAIN_WIDTH = MIX_WIDTH - MEM_WIDTH
RET_HEADS = 6
RET_V_DIM = MAIN_WIDTH // RET_HEADS
RET_QK_DIM = RET_V_DIM // 2
DIFF_HEADS = 6
DIFF_HEAD_DIM = MAIN_WIDTH // (2 * DIFF_HEADS)
DIFF_V_DIM = 2 * DIFF_HEAD_DIM
IN_WIDTH = 3 * MAIN_WIDTH + MEM_WIDTH
FFN_DIM = -(-8 * D_MODEL // (3 * 256)) * 256
EPS = 1e-6


def rms_norm(x, w):
    x32 = x.astype(jnp.float32)
    y = x32 * lax.rsqrt(jnp.mean(x32 * x32, axis=-1, keepdims=True) + EPS)
    return (y * w.astype(jnp.float32)).astype(x.dtype)

def retention(q, k, v):
    B, S, H, dk = q.shape
    dv = v.shape[-1]
    nc = S // CHUNK
    dt = q.dtype
    log_gamma = jnp.log(1.0 - 2.0 ** (-5.0 - jnp.arange(H, dtype=jnp.float32)))
    k = k * (dk ** -0.5)
    q = q.reshape(B, nc, CHUNK, H, dk)
    k = k.reshape(B, nc, CHUNK, H, dk)
    v = v.reshape(B, nc, CHUNK, H, dv)
    pos = jnp.arange(CHUNK, dtype=jnp.float32)
    d_in = jnp.exp(log_gamma[:, None, None] * jnp.abs(pos[:, None] - pos[None, :])).astype(dt)
    s_in = jnp.einsum('bnihd,bnjhd->bnhij', q, k) * d_in
    o_in = jnp.einsum('bnhij,bnjhe->bnihe', s_in, v)
    k_dec = jnp.exp(log_gamma[:, None] * (CHUNK - 1 - pos)[None, :]).astype(dt)
    kv = jnp.einsum('bnjhd,hj,bnjhe->bnhde', k, k_dec, v)
    chunk_dec = jnp.exp(log_gamma * CHUNK).astype(dt)[:, None, None]

    def step(state, kv_c):
        return state * chunk_dec + kv_c, state

    init = jnp.zeros((B, H, dk, dv), dtype=kv.dtype)
    _, prev = lax.scan(step, init, jnp.moveaxis(kv, 1, 0))
    prev = jnp.moveaxis(prev, 0, 1)
    q_dec = jnp.exp(log_gamma[:, None] * (pos + 1.0)[None, :]).astype(dt)
    o_x = jnp.einsum('bnihd,hi,bnhde->bnihe', q, q_dec, prev)
    return (o_in + o_x).reshape(B, S, H, dv)

def diff_attention(q, k, v, lam):
    B, S, H, _, d = q.shape
    nb = S // Q_BLOCK
    slopes = 2.0 ** (-8.0 * jnp.arange(1, H + 1, dtype=jnp.float32) / H)
    s_pos = jnp.arange(S)
    s_chunk = s_pos // CHUNK
    qb = jnp.moveaxis(q.reshape(B, nb, Q_BLOCK, H, 2, d), 1, 0)
    starts = jnp.arange(nb, dtype=jnp.int32) * Q_BLOCK
    scale = d ** -0.5

    def block(args):
        qblk, t0 = args
        t = t0 + jnp.arange(Q_BLOCK)
        sc = jnp.einsum('bihcd,bjhcd->bhcij', qblk, k).astype(jnp.float32) * scale
        dist = jnp.abs(t[:, None] - s_pos[None, :]).astype(jnp.float32)
        bias = -slopes[:, None, None] * dist[None]
        allowed = s_chunk[None, :] <= (t // CHUNK)[:, None]
        sc = jnp.where(allowed, sc + bias[None, :, None], -jnp.inf)
        p = jax.nn.softmax(sc, axis=-1)
        a = p[:, :, 0] - lam * p[:, :, 1]
        return jnp.einsum('bhij,bjhe->bihe', a.astype(v.dtype), v)

    o = lax.map(block, (qb, starts))
    return jnp.moveaxis(o, 0, 1).reshape(B, S, H, v.shape[-1])

def memory_attention(qc, mk, mv):
    sc = jnp.einsum('bshd,bmhd->bhsm', qc, mk).astype(jnp.float32) * (qc.shape[-1] ** -0.5)
    p = jax.nn.softmax(sc, axis=-1).astype(mv.dtype)
    return jnp.einsum('bhsm,bmhd->bshd', p, mv)

def first_inputs(seed: int = 0) -> dict:
    key = jax.random.key(seed)
    ks = jax.random.split(key, 24)
    n = jax.random.normal
    f = jnp.float32

    def gain(k, shape):
        return 1.0 + 0.02 * n(k, shape, f)

    return {
        'x': n(ks[0], (BATCH, SEQ, D_MODEL), f),
        'mem': n(ks[1], (BATCH, MEM_LEN, D_MODEL), f),
        'attn_norm_w': gain(ks[2], (DEPTH, D_MODEL)),
        'w_in': n(ks[3], (DEPTH, D_MODEL, IN_WIDTH), f) * D_MODEL ** -0.5,
        'w_out': n(ks[4], (DEPTH, MIX_WIDTH, D_MODEL), f) * MIX_WIDTH ** -0.5,
        'mem_norm_w': gain(ks[5], (D_MODEL,)),
        'w_mem_kv': n(ks[6], (DEPTH, D_MODEL, 2 * MEM_WIDTH), f) * D_MODEL ** -0.5,
        'mem_q_norm_w': gain(ks[7], (DEPTH, MEM_HEAD_DIM)),
        'mem_k_norm_w': gain(ks[8], (DEPTH, MEM_HEAD_DIM)),
        'ret_gn_w': gain(ks[9], (N_RET_LAYERS, RET_HEADS, RET_V_DIM)),
        'diff_q_norm_w': gain(ks[10], (N_DIFF_LAYERS, DIFF_HEAD_DIM)),
        'diff_k_norm_w': gain(ks[11], (N_DIFF_LAYERS, DIFF_HEAD_DIM)),
        'diff_lambda_q1': 0.1 * n(ks[12], (N_DIFF_LAYERS, DIFF_HEAD_DIM), f),
        'diff_lambda_k1': 0.1 * n(ks[13], (N_DIFF_LAYERS, DIFF_HEAD_DIM), f),
        'diff_lambda_q2': 0.1 * n(ks[14], (N_DIFF_LAYERS, DIFF_HEAD_DIM), f),
        'diff_lambda_k2': 0.1 * n(ks[15], (N_DIFF_LAYERS, DIFF_HEAD_DIM), f),
        'diff_subln_w': gain(ks[16], (N_DIFF_LAYERS, DIFF_V_DIM)),
        'ffn_norm_w': gain(ks[17], (DEPTH, D_MODEL)),
        'w_gate_up': n(ks[18], (DEPTH, D_MODEL, 2 * FFN_DIM), f) * D_MODEL ** -0.5,
        'w_down': n(ks[19], (DEPTH, FFN_DIM, D_MODEL), f) * FFN_DIM ** -0.5,
    }

def first_block(x, mem, attn_norm_w, w_in, w_out, mem_norm_w, w_mem_kv, mem_q_norm_w,
              mem_k_norm_w, ret_gn_w, diff_q_norm_w, diff_k_norm_w, diff_lambda_q1,
              diff_lambda_k1, diff_lambda_q2, diff_lambda_k2, diff_subln_w, ffn_norm_w,
              w_gate_up, w_down):
    B, S, _ = x.shape
    M = mem.shape[1]
    memn = rms_norm(mem, mem_norm_w)
    for layer in range(DEPTH):
        h = rms_norm(x, attn_norm_w[layer])
        u = h @ w_in[layer]
        j = layer // N_MIXERS
        if layer % N_MIXERS == 0:
            nqk = RET_HEADS * RET_QK_DIM
            q = u[..., :nqk].reshape(B, S, RET_HEADS, RET_QK_DIM)
            k = u[..., nqk:2 * nqk].reshape(B, S, RET_HEADS, RET_QK_DIM)
            v = u[..., 2 * nqk:2 * nqk + MAIN_WIDTH].reshape(B, S, RET_HEADS, RET_V_DIM)
            g = u[..., 2 * nqk + MAIN_WIDTH:3 * MAIN_WIDTH]
            o = rms_norm(retention(q, k, v), ret_gn_w[j])
            o_main = jax.nn.silu(g) * o.reshape(B, S, MAIN_WIDTH)
        else:
            q = u[..., :MAIN_WIDTH].reshape(B, S, DIFF_HEADS, 2, DIFF_HEAD_DIM)
            k = u[..., MAIN_WIDTH:2 * MAIN_WIDTH].reshape(B, S, DIFF_HEADS, 2, DIFF_HEAD_DIM)
            v = u[..., 2 * MAIN_WIDTH:3 * MAIN_WIDTH].reshape(B, S, DIFF_HEADS, DIFF_V_DIM)
            q = rms_norm(q, diff_q_norm_w[j])
            k = rms_norm(k, diff_k_norm_w[j])
            lambda_init = 0.8 - 0.6 * math.exp(-0.3 * layer)
            lq1 = diff_lambda_q1[j].astype(jnp.float32)
            lk1 = diff_lambda_k1[j].astype(jnp.float32)
            lq2 = diff_lambda_q2[j].astype(jnp.float32)
            lk2 = diff_lambda_k2[j].astype(jnp.float32)
            lam = jnp.exp(jnp.sum(lq1 * lk1)) - jnp.exp(jnp.sum(lq2 * lk2)) + lambda_init
            o = rms_norm(diff_attention(q, k, v, lam), diff_subln_w[j]) * (1.0 - lambda_init)
            o_main = o.reshape(B, S, MAIN_WIDTH)
        qc = rms_norm(u[..., 3 * MAIN_WIDTH:].reshape(B, S, MEM_HEADS, MEM_HEAD_DIM), mem_q_norm_w[layer])
        mkv = memn @ w_mem_kv[layer]
        mk = rms_norm(mkv[..., :MEM_WIDTH].reshape(B, M, MEM_HEADS, MEM_HEAD_DIM), mem_k_norm_w[layer])
        mv = mkv[..., MEM_WIDTH:].reshape(B, M, MEM_HEADS, MEM_HEAD_DIM)
        o_mem = memory_attention(qc, mk, mv).reshape(B, S, MEM_WIDTH)
        x = x + jnp.concatenate([o_main, o_mem], axis=-1) @ w_out[layer]
        h = rms_norm(x, ffn_norm_w[layer])
        gu = h @ w_gate_up[layer]
        x = x + (jax.nn.silu(gu[..., :FFN_DIM]) * gu[..., FFN_DIM:]) @ w_down[layer]
    return x


DEPTH_2 = 1

N_MEM = 256
GDN_HEAD_DIM = 128
GDN_WIDTH = D_MODEL
GDN_HEADS = GDN_WIDTH // GDN_HEAD_DIM
CONV_WIDTH = 4
GLA_HEADS = 4
GLA_KEY_WIDTH = D_MODEL // 2
GLA_VAL_WIDTH = D_MODEL
GLA_KEY_DIM = GLA_KEY_WIDTH // GLA_HEADS
GLA_VAL_DIM = GLA_VAL_WIDTH // GLA_HEADS
GLA_GATE_RANK = 16
GLA_GATE_TAU = 16.0
XATTN_HEADS = 4
XATTN_HEAD_DIM = D_MODEL // XATTN_HEADS
D_FF = 4 * D_MODEL
NORM_EPS = 1e-6
IN_SIZES = (GDN_WIDTH, GDN_WIDTH, GDN_WIDTH, GDN_WIDTH, GDN_HEADS, GDN_HEADS,
            GLA_KEY_WIDTH, GLA_KEY_WIDTH, GLA_VAL_WIDTH, GLA_VAL_WIDTH, GLA_GATE_RANK,
            D_MODEL, D_MODEL)
IN_WIDTH_2 = 4 * GDN_WIDTH + 2 * GDN_HEADS + 2 * GLA_KEY_WIDTH + 2 * GLA_VAL_WIDTH + GLA_GATE_RANK + 2 * D_MODEL


def rmsnorm(x, g):
    xf = x.astype(jnp.float32)
    y = xf * lax.rsqrt(jnp.mean(xf * xf, axis=-1, keepdims=True) + NORM_EPS)
    return (y * g.astype(jnp.float32)).astype(x.dtype)

def l2norm(x):
    return x * lax.rsqrt(jnp.sum(x * x, axis=-1, keepdims=True) + NORM_EPS)

def causal_depthwise_conv(x, w):
    c = x.shape[-1]
    return lax.conv_general_dilated(
        x, w.astype(x.dtype)[:, None, :], window_strides=(1,),
        padding=[(w.shape[0] - 1, 0)], dimension_numbers=("NWC", "WIO", "NWC"),
        feature_group_count=c)

def to_chunks(t, n_heads):
    b, s, _ = t.shape
    return t.reshape(b, s // CHUNK, CHUNK, n_heads, -1).transpose(0, 3, 1, 2, 4)

def scalar_chunks(t):
    b, s, h = t.shape
    return t.reshape(b, s // CHUNK, CHUNK, h).transpose(0, 3, 1, 2)

def from_chunks(t):
    b, h, n, c, d = t.shape
    return t.transpose(0, 2, 3, 1, 4).reshape(b, n * c, h, d)

def gated_delta_rule_chunked(q, k, v, g, beta):
    dk, dv = k.shape[-1], v.shape[-1]
    idx = jnp.arange(CHUNK)
    strict = idx[:, None] > idx[None, :]
    incl = idx[:, None] >= idx[None, :]
    gc = jnp.cumsum(g, axis=-1)
    decay = jnp.exp(jnp.where(incl, gc[..., :, None] - gc[..., None, :], -jnp.inf))
    kk = jnp.einsum('bhnid,bhnjd->bhnij', k, k)
    lower = jnp.where(strict, beta[..., :, None] * kk * decay, 0.0)
    rhs = jnp.concatenate([beta[..., None] * v, (beta * jnp.exp(gc))[..., None] * k], axis=-1)
    sol = lax.linalg.triangular_solve(lower, rhs, left_side=True, lower=True, unit_diagonal=True)
    u, w = sol[..., :dv], sol[..., dv:]
    a_qk = jnp.einsum('bhnid,bhnjd->bhnij', q, k) * decay
    q_dec = q * jnp.exp(gc)[..., None]
    k_dec = k * jnp.exp(gc[..., -1:] - gc)[..., None]
    g_end = jnp.exp(gc[..., -1])
    xs = tuple(jnp.moveaxis(t, 2, 0) for t in (u, w, q_dec, a_qk, k_dec, g_end))

    def step(state, inp):
        u_c, w_c, q_c, a_c, k_c, ge = inp
        delta = u_c - jnp.einsum('bhcd,bhde->bhce', w_c, state)
        o = jnp.einsum('bhcd,bhde->bhce', q_c, state) + jnp.einsum('bhij,bhje->bhie', a_c, delta)
        state = ge[..., None, None] * state + jnp.einsum('bhcd,bhce->bhde', k_c, delta)
        return state, o

    s0 = jnp.zeros(q.shape[:2] + (dk, dv), q.dtype)
    _, o = lax.scan(step, s0, xs)
    return jnp.moveaxis(o, 0, 2)

def gla_chunked(q, k, v, gk):
    dk, dv = k.shape[-1], v.shape[-1]
    idx = jnp.arange(CHUNK)
    incl = idx[:, None] >= idx[None, :]
    bc = jnp.cumsum(gk, axis=-2)
    b_ref = bc[..., CHUNK // 2:CHUNK // 2 + 1, :]
    a_qk = jnp.einsum('bhnid,bhnjd->bhnij', q * jnp.exp(bc - b_ref), k * jnp.exp(b_ref - bc))
    o_intra = jnp.einsum('bhnij,bhnje->bhnie', jnp.where(incl, a_qk, 0.0), v)
    q_dec = q * jnp.exp(bc)
    k_dec = k * jnp.exp(bc[..., -1:, :] - bc)
    g_end = jnp.exp(bc[..., -1, :])
    xs = tuple(jnp.moveaxis(t, 2, 0) for t in (q_dec, o_intra, k_dec, v, g_end))

    def step(state, inp):
        q_c, oi_c, k_c, v_c, ge = inp
        o = jnp.einsum('bhcd,bhde->bhce', q_c, state) + oi_c
        state = ge[..., :, None] * state + jnp.einsum('bhcd,bhce->bhde', k_c, v_c)
        return state, o

    s0 = jnp.zeros(q.shape[:2] + (dk, dv), q.dtype)
    _, o = lax.scan(step, s0, xs)
    return jnp.moveaxis(o, 0, 2)

def second_inputs(seed: int = 0) -> dict:
    key = jax.random.key(seed)
    ks = iter(jax.random.split(key, 32))
    nrm = lambda shape, scale: jax.random.normal(next(ks), shape, jnp.float32) * scale
    gain = lambda n: 1.0 + nrm((DEPTH_2, n), 0.02)
    a_log = jnp.log(jax.random.uniform(next(ks), (DEPTH_2, GDN_HEADS), jnp.float32, 1.0, 16.0))
    dt = jnp.exp(jax.random.uniform(next(ks), (DEPTH_2, GDN_HEADS), jnp.float32, np.log(1e-3), np.log(1e-1)))
    dt_bias = dt + jnp.log(-jnp.expm1(-dt))
    return {
        "x": nrm((BATCH, SEQ, D_MODEL), 1.0),
        "mem": nrm((BATCH, N_MEM, D_MODEL), 1.0),
        "norm_mix_g": gain(D_MODEL),
        "w_in": nrm((DEPTH_2, D_MODEL, IN_WIDTH_2), D_MODEL ** -0.5),
        "gdn_conv_w": nrm((DEPTH_2, CONV_WIDTH, 3 * GDN_WIDTH), CONV_WIDTH ** -0.5),
        "gdn_a_log": a_log,
        "gdn_dt_bias": dt_bias,
        "gdn_norm_g": gain(GDN_HEAD_DIM),
        "gla_w_gate2": nrm((DEPTH_2, GLA_GATE_RANK, GLA_KEY_WIDTH), GLA_GATE_RANK ** -0.5),
        "gla_b_gate": nrm((DEPTH_2, GLA_KEY_WIDTH), 0.1),
        "gla_norm_g": gain(GLA_VAL_DIM),
        "w_branch_gdn": nrm((DEPTH_2, GDN_WIDTH, D_MODEL), GDN_WIDTH ** -0.5),
        "w_branch_gla": nrm((DEPTH_2, GLA_VAL_WIDTH, D_MODEL), GLA_VAL_WIDTH ** -0.5),
        "w_out": nrm((DEPTH_2, D_MODEL, D_MODEL), D_MODEL ** -0.5),
        "norm_xattn_g": gain(D_MODEL),
        "norm_mem_g": gain(D_MODEL),
        "xattn_wq": nrm((DEPTH_2, D_MODEL, D_MODEL), D_MODEL ** -0.5),
        "xattn_wk": nrm((DEPTH_2, D_MODEL, D_MODEL), D_MODEL ** -0.5),
        "xattn_wv": nrm((DEPTH_2, D_MODEL, D_MODEL), D_MODEL ** -0.5),
        "xattn_wo": nrm((DEPTH_2, D_MODEL, D_MODEL), D_MODEL ** -0.5),
        "norm_mlp_g": gain(D_MODEL),
        "mlp_w1": nrm((DEPTH_2, D_MODEL, D_FF), D_MODEL ** -0.5),
        "mlp_w2": nrm((DEPTH_2, D_FF, D_MODEL), D_FF ** -0.5),
        "norm_final_g": 1.0 + nrm((D_MODEL,), 0.02),
    }

def second_block(x, mem, norm_mix_g, w_in, gdn_conv_w, gdn_a_log, gdn_dt_bias, gdn_norm_g,
              gla_w_gate2, gla_b_gate, gla_norm_g, w_branch_gdn, w_branch_gla, w_out,
              norm_xattn_g, norm_mem_g, xattn_wq, xattn_wk, xattn_wv, xattn_wo,
              norm_mlp_g, mlp_w1, mlp_w2, norm_final_g):
    dt = x.dtype
    f32 = jnp.float32
    bsz, seq, _ = x.shape
    split_at = [int(v) for v in np.cumsum(IN_SIZES)[:-1]]
    for i in range(DEPTH_2):
        h = rmsnorm(x, norm_mix_g[i])
        proj = h @ w_in[i].astype(dt)
        (gq, gk_, gv, gz, ga, gb, lq, lk, lv, lr, lgate, gate_a, gate_b) = jnp.split(proj, split_at, axis=-1)

        qkv = jax.nn.silu(causal_depthwise_conv(jnp.concatenate([gq, gk_, gv], -1), gdn_conv_w[i]))
        cq, ck, cv = jnp.split(qkv.astype(f32), [GDN_WIDTH, 2 * GDN_WIDTH], axis=-1)
        q_a = l2norm(to_chunks(cq, GDN_HEADS)) * (GDN_HEAD_DIM ** -0.5)
        k_a = l2norm(to_chunks(ck, GDN_HEADS))
        v_a = to_chunks(cv, GDN_HEADS)
        g_a = -jnp.exp(gdn_a_log[i].astype(f32)) * jax.nn.softplus(ga.astype(f32) + gdn_dt_bias[i].astype(f32))
        beta_a = jax.nn.sigmoid(gb.astype(f32))
        o_a = gated_delta_rule_chunked(q_a, k_a, v_a, scalar_chunks(g_a), scalar_chunks(beta_a))
        o_a = rmsnorm(from_chunks(o_a).astype(dt), gdn_norm_g[i]) * jax.nn.silu(gz.reshape(bsz, seq, GDN_HEADS, GDN_HEAD_DIM))
        y_a = o_a.reshape(bsz, seq, GDN_WIDTH) @ w_branch_gdn[i].astype(dt)

        log_fg = jax.nn.log_sigmoid((lgate @ gla_w_gate2[i].astype(dt)).astype(f32) + gla_b_gate[i].astype(f32)) / GLA_GATE_TAU
        q_b = to_chunks(lq.astype(f32), GLA_HEADS) * (GLA_KEY_DIM ** -0.5)
        k_b = to_chunks(lk.astype(f32), GLA_HEADS)
        v_b = to_chunks(lv.astype(f32), GLA_HEADS)
        o_b = gla_chunked(q_b, k_b, v_b, to_chunks(log_fg, GLA_HEADS))
        o_b = rmsnorm(from_chunks(o_b).astype(dt), gla_norm_g[i]) * jax.nn.silu(lr.reshape(bsz, seq, GLA_HEADS, GLA_VAL_DIM))
        y_b = o_b.reshape(bsz, seq, GLA_VAL_WIDTH) @ w_branch_gla[i].astype(dt)

        merged = jax.nn.sigmoid(gate_a) * y_a + jax.nn.sigmoid(gate_b) * y_b
        x = x + merged @ w_out[i].astype(dt)

        h = rmsnorm(x, norm_xattn_g[i])
        m = rmsnorm(mem.astype(dt), norm_mem_g[i])
        q = (h @ xattn_wq[i].astype(dt)).reshape(bsz, seq, XATTN_HEADS, XATTN_HEAD_DIM)
        k = (m @ xattn_wk[i].astype(dt)).reshape(bsz, -1, XATTN_HEADS, XATTN_HEAD_DIM)
        v = (m @ xattn_wv[i].astype(dt)).reshape(bsz, -1, XATTN_HEADS, XATTN_HEAD_DIM)
        s = jnp.einsum('bshd,bmhd->bhsm', q, k).astype(f32) * (XATTN_HEAD_DIM ** -0.5)
        p = jax.nn.softmax(s, axis=-1).astype(dt)
        o = jnp.einsum('bhsm,bmhd->bshd', p, v).reshape(bsz, seq, D_MODEL)
        x = x + o @ xattn_wo[i].astype(dt)

        h = rmsnorm(x, norm_mlp_g[i])
        x = x + jnp.square(jax.nn.relu(h @ mlp_w1[i].astype(dt))) @ mlp_w2[i].astype(dt)
    return rmsnorm(x, norm_final_g)


def setup_inputs(seed=0):
    out = dict(first_inputs(seed))
    for name, value in second_inputs(seed + 1).items():
        if name != "x":
            out[name + "_2"] = value
    return out


def reference(
    x, mem, attn_norm_w, w_in, w_out, mem_norm_w, w_mem_kv, mem_q_norm_w, mem_k_norm_w,
    ret_gn_w, diff_q_norm_w, diff_k_norm_w, diff_lambda_q1, diff_lambda_k1, diff_lambda_q2,
    diff_lambda_k2, diff_subln_w, ffn_norm_w, w_gate_up, w_down, mem_2, norm_mix_g_2, w_in_2,
    gdn_conv_w_2, gdn_a_log_2, gdn_dt_bias_2, gdn_norm_g_2, gla_w_gate2_2, gla_b_gate_2,
    gla_norm_g_2, w_branch_gdn_2, w_branch_gla_2, w_out_2, norm_xattn_g_2, norm_mem_g_2,
    xattn_wq_2, xattn_wk_2, xattn_wv_2, xattn_wo_2, norm_mlp_g_2, mlp_w1_2, mlp_w2_2,
    norm_final_g_2,
):
    x = first_block(
        x, mem, attn_norm_w, w_in, w_out, mem_norm_w, w_mem_kv, mem_q_norm_w, mem_k_norm_w,
        ret_gn_w, diff_q_norm_w, diff_k_norm_w, diff_lambda_q1, diff_lambda_k1, diff_lambda_q2,
        diff_lambda_k2, diff_subln_w, ffn_norm_w, w_gate_up, w_down,
    )
    return second_block(
        x, mem_2, norm_mix_g_2, w_in_2, gdn_conv_w_2, gdn_a_log_2, gdn_dt_bias_2, gdn_norm_g_2,
        gla_w_gate2_2, gla_b_gate_2, gla_norm_g_2, w_branch_gdn_2, w_branch_gla_2, w_out_2,
        norm_xattn_g_2, norm_mem_g_2, xattn_wq_2, xattn_wk_2, xattn_wv_2, xattn_wo_2,
        norm_mlp_g_2, mlp_w1_2, mlp_w2_2, norm_final_g_2,
    )


_drawn_inputs = setup_inputs


def setup_inputs(seed=0):
    import zlib

    import numpy as np

    out = dict(_drawn_inputs(seed))
    spreads = {}
    factors = {'mem_norm_w': 8.0,
     'mem_q_norm_w': 8.0,
     'mem_k_norm_w': 8.0,
     'ret_gn_w': 3.988,
     'diff_q_norm_w': 5.066,
     'diff_k_norm_w': 5.361,
     'diff_lambda_q2': 8.0,
     'diff_subln_w': 5.332,
     'norm_mix_g_2': 4.913,
     'gdn_norm_g_2': 8.0,
     'gla_b_gate_2': 6.62,
     'gla_norm_g_2': 8.0,
     'norm_xattn_g_2': 8.0,
     'norm_mem_g_2': 8.0,
     'norm_mlp_g_2': 16.616,
     'norm_final_g_2': 8.102}
    for name, (base, spread) in spreads.items():
        noise = np.random.default_rng([zlib.crc32(name.encode()), seed]).standard_normal(out[name].shape)
        drawn = base * np.exp(spread * noise) if base else spread * noise
        out[name] = __import__('jax').numpy.asarray(drawn.astype(out[name].dtype))
    for name, factor in factors.items():
        out[name] = (out[name] * factor).astype(out[name].dtype)
    return out
```

```python
import math
from contextlib import ExitStack

import numpy as np

import concourse.bass as bass
from concourse import mybir

F32 = mybir.dt.float32
F32R = mybir.dt.float32r
ACT = mybir.ActivationFunctionType
ALU = mybir.AluOpType
AX = mybir.AxisListType

P = 128
T = 256
D = 1024
EPS = 1e-6
FFN = 2816
MIX = 768
UW = 1024
NR = 4
NH = 6
LA = 4
NSLOT = 19
LAMBDA_INIT = 0.8 - 0.6 * math.exp(-0.3)

GAINS = ["attn0", "attn1", "ffn0", "ffn1", "mem", "mix2", "xattn", "mem2", "mlp", "final"]
ROWS = {"ret_gn": (0, 768), "subln": (768, 128), "gdn_g": (896, 128), "gla_g": (1024, 256),
        "a_log": (1280, 8), "dt_bias": (1288, 8), "lq1": (1296, 64), "lk1": (1360, 64),
        "lq2": (1424, 64), "lk2": (1488, 64)}
NROW = 1552
VECS = {"conv": (0, 96), "b_gate": (96, 4), "dq": (100, 1), "dk": (101, 1), "mq": (102, 2), "mk": (104, 2)}
NVEC = 106
CONS = {"ident": (0, 128), "U": (128, 128), "S": (256, 128), "CO": (384, 256), "LM": (640, 768)}
NCON = 1408


def shape_constants():
    i = np.arange(128)
    same = (i[:, None] // 64) == (i[None, :] // 64)
    con = np.zeros((128, NCON), np.float32)
    con[:, 0:128] = np.eye(128)
    con[:, 128:256] = (i[:, None] <= i[None, :]) & same
    con[:, 256:384] = (i[:, None] > i[None, :]) & same
    for c in range(2):
        con[:, 384 + 128 * c:512 + 128 * c] = ((i // 64) == c)[:, None]
    for n in range(6):
        s = 1 << n
        blk = (i[:, None] // (2 * s) == i[None, :] // (2 * s)) & (i[:, None] // s % 2 == 0) & (i[None, :] // s % 2 == 1)
        con[:, 640 + 128 * n:768 + 128 * n] = blk
    pos = np.arange(256)
    dist = np.abs(pos[:, None] - pos[None, :]).astype(np.float64)
    seen = (pos[None, :] // 64) <= (pos[:, None] // 64)
    ret = np.zeros((128, 6, 384), np.float32)
    dif = np.zeros((128, 6, 384), np.float32)
    for h in range(6):
        lg = math.log(1.0 - 2.0 ** (-5.0 - h))
        dm = np.where(seen, np.exp(lg * dist), 0.0).T * 64 ** -0.5
        ret[:, h, 0:256] = dm[0:128, :]
        ret[:, h, 256:384] = dm[128:256, 128:256]
        slope = 2.0 ** (-8.0 * (h + 1) / 6)
        b = np.where(seen, -slope * dist, -1e30)
        dif[:, h, 0:128] = b[0:128, 0:128]
        dif[:, h, 128:384] = b[128:256, :]
    return con, ret.reshape(128, 2304), dif.reshape(128, 2304)


class Queue:

    def __init__(self, eng, sem, dry):
        self.eng, self.sem, self.n, self.seen, self.dry = eng, sem, 0, {}, dry

    def wait(self, toks):
        for t in toks:
            if t is None:
                continue
            if isinstance(t, list):
                self.wait(t)
            elif self.seen.get(id(t[0]), 0) < t[1]:
                self.seen[id(t[0])] = t[1]
                if not self.dry:
                    self.eng.wait_ge(t[0], t[1])

    def __call__(self, fn, *toks, sig=True):
        self.wait(toks)
        if sig:
            self.n += 1
        if not self.dry:
            ins = fn(self.eng)
            if sig:
                ins.then_inc(self.sem, 1)
        return (self.sem, self.n)

    def dma(self, fn, sem, value, *toks):
        self.wait(toks)
        if not self.dry:
            fn(self.eng).then_inc(sem, 16)
        return (sem, value)


def build(nc, W, out, plan, stop=99):
    dry = plan is None
    order = []
    peaks = []
    ctx = ExitStack()
    with ctx:
        sb = lambda n, s, d=F32: ctx.enter_context(nc.sbuf_tensor(n, s, d))
        sem = lambda n: ctx.enter_context(nc.semaphore(n))
        tag = "d" if dry else ""
        raw = sb(tag + "raw", [P, NR, UW])
        spl = sb(tag + "spl", [P, NH, 2, UW], F32R)
        X = sb(tag + "X", [P, 2, D])
        xs = sb(tag + "xs", [P, 2, 8, T], F32R)
        ys = sb(tag + "ys", [P, 2, 8, T], F32R)
        gain = sb(tag + "gain", [P, 1, D])
        con = sb(tag + "con", [P, NCON])
        row = sb(tag + "row", [P, NROW])
        vec = sb(tag + "vec", [P, NVEC])
        sml = sb(tag + "sml", [P, 1536])
        gl2 = sb(tag + "gl2", [16, 512])
        sraw = sb(tag + "sraw", [P, 8, 32])
        sspl = sb(tag + "sspl", [P, 2, 8, 32], F32R)
        ar = sb(tag + "ar", [P, NSLOT, 1024])
        ps = [ctx.enter_context(nc.psum_tensor(f"{tag}ps{i}", [P, 512], F32)) for i in range(8)]

        PE = Queue(nc.tensor, sem(tag + "s_pe"), dry)
        AC = Queue(nc.scalar, sem(tag + "s_act"), dry)
        DV = Queue(nc.vector, sem(tag + "s_dve"), dry)
        PO = Queue(nc.gpsimd, sem(tag + "s_pool"), dry)
        SP = Queue(nc.sync, None, dry)
        s_raw = [sem(f"{tag}s_raw{i}") for i in range(NR)]
        s_ld = [sem(f"{tag}s_ld{i}") for i in range(40)]
        s_out = sem(tag + "s_out")
        ld = [0]

        def load(dst, src, *toks, q=None):
            s = s_ld[ld[0]]
            ld[0] += 1
            return (q or PO).dma(lambda e: e.dma_start(dst, src), s, 16, *toks)

        sm = [0]

        def small(n):
            a = sm[0]
            sm[0] += n
            assert sm[0] <= 1536
            return sml[:, a:a + n]

        slots = [(0, []) for i in range(40)] if dry else [(i, []) for i in range(NSLOT)]
        peak = [0]

        class Slot:

            def __init__(self):
                self.i, self.free = slots.pop(0)
                peak[0] = max(peak[0], (40 if dry else NSLOT) - len(slots))
                self.v = ar[:, self.i, :]
                self.v2 = ar[:, self.i, :].rearrange("p (t n) -> p t n", t=2)

            def give(self, *toks):
                slots.append((self.i, list(toks)))

        banks = [(i, []) for i in range(8)]

        class Bank:

            def __init__(self):
                self.i, self.free = banks.pop(0)
                self.v = ps[self.i][:, :]

            def g(self, n):
                return ps[self.i][:, :].rearrange("p (a b) -> p a b", a=n)

            def give(self, *toks):
                banks.append((self.i, list(toks)))

        t_con = load(con[:, :], W["con"])
        t_row = load(row[:, :], W["rows"].partition_broadcast(P))
        t_vec = load(vec[:, :], W["vecs"])
        ident = con[:, 0:128]
        cU = con[:, 128:256]
        cS = con[:, 256:384]
        R = lambda n: row[:, ROWS[n][0]:ROWS[n][0] + ROWS[n][1]]
        V = lambda n, k=0, w=1: vec[:, VECS[n][0] + k:VECS[n][0] + k + w]
        xin = lambda a: a.rearrange("b (t p) d -> p (b t) d", p=P)
        neg = small(32)
        t_neg = PO(lambda e: e.memset(neg, -0.5))

        def bc(ap, n):
            return ap.unsqueeze(ap.ndim).to_broadcast(list(ap.shape) + [n])

        def bm(ap, n):
            return ap.unsqueeze(1).to_broadcast([ap.shape[0], n] + list(ap.shape[1:]))

        raw_tok, lo_tok, pe_tok, cnt = {}, {}, {}, [0] * NR
        nsplit = [0]

        def fetch(u, *toks):
            s = u % NR
            src = plan[u]
            if len(src.shape) == 4:
                dst = raw[:, s, :].rearrange("p (a b c) -> p a b c", a=src.shape[1], b=2)
                parts = [(dst[:, :, i, :], src[:, :, i, :]) for i in range(2)]
            else:
                parts = [(raw[:, s, :].rearrange("p (a b) -> p a b", a=2), src)]
            for dst, src in parts:
                cnt[s] += 16
                raw_tok[u] = SP.dma(lambda e: e.dma_start(dst, src), s_raw[s], cnt[s], *toks)

        def split(u):
            s, h = u % NR, u % NH
            a = AC(lambda e: e.copy(spl[:, h, 0, :], raw[:, s, :]), raw_tok[u], pe_tok.get(u - NH))
            lo_tok[u] = DV(lambda e: e.tensor_tensor(spl[:, h, 1, :], raw[:, s, :],
                                                     spl[:, h, 0, :].bitcast(F32), ALU.subtract), a)
            if u + NR < len(plan):
                fetch(u + NR, lo_tok[u])

        def unit(src):
            u = len(order)
            order.append(src)
            if not dry:
                while nsplit[0] < min(u + 1 + LA, len(plan)):
                    split(nsplit[0])
                    nsplit[0] += 1
            v = spl[:, u % NH, :, :].rearrange("p l (a b) -> p l a b", a=2)
            return u, v[:, 0], v[:, 1]

        def product(u, xin_, kt, t, w_hi, w_lo, bank, start, stop, last):
            xh, xl = xin_[:, 0, kt, t * P:(t + 1) * P], xin_[:, 1, kt, t * P:(t + 1) * P]
            PE(lambda e: e.matmul(bank, xh, w_hi, start=start, stop=False), lo_tok.get(u), sig=False)
            PE(lambda e: e.matmul(bank, xh, w_lo, start=False, stop=False), sig=False)
            return PE(lambda e: e.matmul(bank, xl, w_hi, start=False, stop=stop), sig=last)

        def cols(src_of, xin_, xtok, done):
            b = [Bank(), Bank()]
            for k in range(4):
                u, hi, lo = unit(src_of(k))
                for j in range(2):
                    kt = 2 * k + j
                    for t in range(2):
                        if kt == 0:
                            PE.wait([b[t].free, xtok])
                        tok = product(u, xin_, kt, t, hi[:, j], lo[:, j], b[t].v, kt == 0, kt == 7,
                                      j == 1 and t == 1)
                pe_tok[u] = tok
                if k == 3:
                    done(b, tok)
                yield

        def rows_(w, kts, xin_, off, xtok, acc, first, last):
            for n, kt in enumerate(kts):
                u, hi, lo = unit(w[kt * P:(kt + 1) * P, :].rearrange("p (a b) -> p a b", a=2))
                for t in range(2):
                    for j in range(2):
                        if n == 0:
                            PE.wait([acc[t][j].free, xtok])
                        tok = product(u, xin_, off + n, t, hi[:, j], lo[:, j], acc[t][j].v,
                                      first and n == 0, last and n == len(kts) - 1, t == 1 and j == 1)
                pe_tok[u] = tok
                yield tok

        def block(w, c0):
            return lambda k: w[k * 256:(k + 1) * 256, c0:c0 + 512].rearrange("(a p) n -> p a n", p=P)

        def run(g):
            for _ in g:
                pass

        def chain(*gs):
            for g in gs:
                yield from g

        def weave(main, bg, n=1):
            for _ in main:
                for _ in range(n):
                    next(bg, None)
            run(bg)

        xuse = {id(xs): [], id(ys): []}

        def halves(src, dst, k0, nk, t, *toks):
            b = Bank()
            PE.wait([b.free])
            for j in range(nk):
                tok = PE(lambda e, j=j: e.transpose(b.v[:, j * P:(j + 1) * P], src[:, j * P:(j + 1) * P], ident),
                         *toks, t_con, sig=(j == nk - 1))
            bv = b.g(4)[:, 0:nk, :]
            o = lambda l: dst[:, l, k0:k0 + nk, t * P:(t + 1) * P]
            a = AC(lambda e: e.copy(o(0), bv), tok, *xuse[id(dst)])
            d = DV(lambda e: e.tensor_tensor(o(1), bv, o(0).bitcast(F32), ALU.subtract), a)
            b.give(d)
            return d

        def spread(srcs, dst, toks):
            r = []
            for t in range(2):
                for k in range(2):
                    r.append(halves(srcs[t][:, k * 512:(k + 1) * 512], dst, 4 * k, 4, t, toks[t]))
            xuse[id(dst)] = []
            return r

        ng = [0]
        guse = [[]]

        def get_gain(name):
            i = 0
            ng[0] += 1
            return i, load(gain[:, i, :], W["gains"][GAINS.index(name):GAINS.index(name) + 1, :]
                           .partition_broadcast(P), guse[i])

        def rsqrt(ss, n, scale, eps, tok):
            m, r = small(n), small(n)
            a = DV(lambda e: e.tensor_scalar(m, ss, scale, eps, ALU.mult, ALU.add), tok)
            return r, PO(lambda e: e.tensor_tensor(r, m, neg[:, 0:n], ALU.pow), a, t_neg)

        def norm(src, g, dst, stoks, yields=True):
            gi, gt = g
            hb = [Slot(), Slot()]
            ht = []
            for t in range(2):
                ss = small(1)
                a = AC(lambda e: e.activation(hb[t].v, src(t), ACT.Square, accum_out=ss), stoks[t], hb[t].free)
                r, rt = rsqrt(ss, 1, 1.0 / D, EPS, a)
                ht.append(DV(lambda e: e.scalar_tensor_tensor(hb[t].v, src(t), r, gain[:, gi, :],
                                                              ALU.mult, ALU.mult), rt, gt))
            guse[gi] = [ht[-1]]
            res = spread([hb[0].v, hb[1].v], dst, ht)
            for t in range(2):
                hb[t].give(res[-1], (PE.sem, PE.n))
            return res

        def evac(dst_of, eng=AC):
            out_ = {}

            def done(b, tok):
                for t in range(2):
                    dst, w = dst_of(t)
                    if eng is AC:
                        a = AC(lambda e: e.copy(dst, b[t].v), tok, w)
                    else:
                        a = DV(lambda e: e.tensor_copy(dst, b[t].v), tok, w)
                    b[t].give(a)
                    out_[t] = a
            return done, out_

        def to_slot(src_of, xin_, xtok, box):
            def g():
                s = Slot()
                done, o = evac(lambda t: (s.v2[:, t, :], s.free))
                yield from cols(src_of, xin_, xtok, done)
                box.append((s, [o[0], o[1]]))
            return g()

        def residual(w, nk, xin_, xtok, xt):
            acc = [[Bank(), Bank()], [Bank(), Bank()]]
            for tok in rows_(w, range(nk), xin_, 0, xtok, acc, True, True):
                yield
            add_acc(acc, tok, xt)

        def add_acc(acc, tok, xt):
            for t in range(2):
                for j in range(2):
                    v = X[:, t, j * 512:(j + 1) * 512]
                    a = DV(lambda e: e.tensor_tensor(v, acc[t][j].v, v, ALU.add), tok, xt[t])
                    acc[t][j].give(a)
                xt[t] = a

        def group_rs(v, n, w, scale, eps, tok, mul=None):
            s = Slot()
            sq = s.v[:, 0:n * w]
            p = PO(lambda e: e.tensor_tensor(sq, v, v, ALU.mult), tok, s.free)
            ss = small(n)
            d = DV(lambda e: e.tensor_reduce(ss, sq.rearrange("p (a b) -> p a b", b=w), AX.X, ALU.add), p)
            s.give(d)
            r, rt = rsqrt(ss, n, scale, eps, d)
            if mul is not None:
                r2 = small(n)
                rt = DV(lambda e: e.tensor_scalar(r2, r, mul, None, ALU.mult), rt)
                r = r2
            return r, rt

        def softmax_mem(t, sc, toks_b, n):
            s = Slot()
            m, nm, sm_, r = small(4), small(4), small(4), small(4)
            done = []
            for i, b in enumerate(sc):
                d = DV(lambda e: e.tensor_reduce(m[:, 2 * i:2 * i + 2], b.g(2), AX.X, ALU.max), toks_b[i])
                d = DV(lambda e: e.tensor_scalar(nm[:, 2 * i:2 * i + 2], m[:, 2 * i:2 * i + 2], -1.0, None,
                                                 ALU.mult), d)
                for k in range(2):
                    h = 2 * i + k
                    a = AC(lambda e: e.activation(s.v[:, h * 256:(h + 1) * 256], b.g(2)[:, k, :], ACT.Exp,
                                                  bias=nm[:, h:h + 1], accum_out=sm_[:, h:h + 1]), d, s.free)
                b.give(a)
            d = DV(lambda e: e.reciprocal(r, sm_), a)
            v = s.v.rearrange("p (h n) -> p h n", h=4)
            d = DV(lambda e: e.tensor_tensor(v, v, bc(r, 256), ALU.mult), d)
            return s, d

        def transposed8(src, tok, dst, dfree, eng2=True):
            r = []
            for k in range(2):
                b = Bank()
                PE.wait([b.free, tok, t_con])
                for j in range(4):
                    p = PE(lambda e: e.transpose(b.v[:, j * P:(j + 1) * P],
                                                 src[:, (4 * k + j) * P:(4 * k + j + 1) * P], ident), sig=(j == 3))
                if k == 0:
                    a = AC(lambda e: e.copy(dst[:, k * 512:(k + 1) * 512], b.v), p, dfree)
                else:
                    a = DV(lambda e: e.tensor_copy(dst[:, k * 512:(k + 1) * 512], b.v), p, dfree)
                b.give(a)
                r.append(a)
            return r

        def mem_attention(qc, qtok, kT, v, ktok, O, Otok, wq):
            wcol = small(1)
            wt = DV(lambda e: e.tensor_scalar(wcol, wq, 0.125, None, ALU.mult), t_vec)
            s = Slot()
            b = Bank()
            ht = []
            for t in range(2):
                r, rt = group_rs(qc(t), 4, 64, 1.0 / 64, EPS, qtok[t])
                hv = s.v[:, t * 256:(t + 1) * 256].rearrange("p (a b) -> p a b", b=64)
                ht.append(DV(lambda e: e.tensor_tensor(hv, qc(t).rearrange("p (a b) -> p a b", b=64), bc(r, 64),
                                                       ALU.mult), rt, s.free))
            yield
            for t in range(2):
                for f in range(2):
                    PE.wait([b.free, ht[t], t_con])
                    p = PE(lambda e: e.transpose(b.v[:, f * 256 + t * P:f * 256 + (t + 1) * P],
                                                 s.v[:, t * 256 + f * P:t * 256 + (f + 1) * P], ident),
                           sig=(t == 1 and f == 1))
            qT = s.v[:, 512:1024]
            a = AC(lambda e: e.mul(qT, b.v, wcol), p, wt)
            b.give(a)
            yield
            for t in range(2):
                sc, st = [], []
                for k in range(2):
                    b = Bank()
                    sc.append(b)
                    p0 = 64 * k
                    for f in range(2):
                        PE.wait([b.free, a, ktok])
                        p = PE(lambda e: e.matmul(b.g(2)[:, f, :], qT[p0:p0 + 64, f * 256 + t * P:f * 256 + (t + 1) * P],
                                                  kT[p0:p0 + 64, f, :], start=True, stop=True), sig=(f == 1))
                    st.append(p)
                w, wtok = softmax_mem(t, sc, st, 256)
                yield
                yield
                wT = Slot()
                tt = transposed8(w.v, wtok, wT.v, wT.free)
                w.give((PE.sem, PE.n))
                yield
                ob = Bank()
                nh = lambda h: 2 * (h % 2) + h // 2
                for h in range(4):
                    for m in range(2):
                        PE.wait([ob.free, tt])
                        p = PE(lambda e: e.matmul(ob.v[:, h * 64:(h + 1) * 64],
                                                  wT.v[:, (2 * nh(h) + m) * P:(2 * nh(h) + m + 1) * P],
                                                  v(m)[:, h * 64:(h + 1) * 64], start=(m == 0), stop=(m == 1)),
                               sig=(h == 3 and m == 1))
                wT.give(p)
                o = AC(lambda e: e.copy(O[t].v[:, 768:1024], ob.v[:, 0:256]), p, O[t].free)
                ob.give(o)
                Otok[t].append(o)
            s.give(p)

        def mem_keys(box, kv, wk):
            s, tk = kv
            ht = []
            for t in range(2):
                kk = s.v2[:, t, 0:256]
                r, rt = group_rs(kk, 4, 64, 1.0 / 64, EPS, tk[t])
                v3 = kk.rearrange("p (a b) -> p a b", b=64)
                ht.append(DV(lambda e: e.tensor_tensor(v3, v3, bc(r, 64), ALU.mult), rt))
            yield
            b = Bank()
            for t in range(2):
                for f in range(2):
                    PE.wait([b.free, ht[t], t_con])
                    p = PE(lambda e: e.transpose(b.v[:, f * 256 + t * P:f * 256 + (t + 1) * P],
                                                 s.v2[:, t, f * P:(f + 1) * P], ident), sig=(t == 1 and f == 1))
            a = AC(lambda e: e.mul(s.v2[:, :, 0:256], b.g(2), wk), p, t_vec)
            b.give(a)
            box.append(a)
            yield

        def out_norm(O, Otok, n, w, grow, mul, gate=None):
            for t in range(2):
                ov = O[t].v[:, 0:n * w]
                o3 = ov.rearrange("p (a b) -> p a b", b=w)
                r, rt = group_rs(ov, n, w, 1.0 / w, EPS, Otok[t], mul)
                d = DV(lambda e: e.tensor_tensor(o3, o3, bc(r, w), ALU.mult), rt)
                p = PO(lambda e: e.tensor_tensor(o3, o3, grow, ALU.mult), d, t_row)
                if gate is not None:
                    p = gate(t, p)
                Otok[t].append(p)
                yield

        x_tok = load(X[:, :, :], xin(W["x"]), q=SP)
        mem_s = [Slot(), Slot()]
        m_tok = [load(mem_s[t].v, W["mem"][0, t * P:(t + 1) * P, :], q=SP) for t in range(2)]
        if not dry:
            for u in range(min(NR, len(plan))):
                fetch(u)
        xt = [x_tok, x_tok]

        mtok = norm(lambda t: mem_s[t].v, get_gain("mem"), ys, m_tok)
        for t in range(2):
            mem_s[t].give((DV.sem, DV.n), (PE.sem, PE.n))
        xtok = norm(lambda t: X[:, t, :], get_gain("attn0"), xs, xt)

        kvs, mks = [], []
        run(to_slot(block(W["w_mem_kv"][0], 0), ys, mtok, kvs))
        weave(to_slot(block(W["w_mem_kv"][1], 0), ys, mtok, kvs), mem_keys(mks, kvs[0], V("mk", 0)))
        xuse[id(ys)] = [(PE.sem, PE.n)]

        def out_banks(o_of, O, Otok, hp):
            b = Bank()
            for k in range(2):
                o_of(b, 2 * hp + k, k)
            tok = (PE.sem, PE.n)
            bv = b.v.rearrange("p (k t n) -> p k t n", k=2, t=2)
            for t in range(2):
                o = O[t].v[:, hp * 256:(hp + 1) * 256].rearrange("p (k n) -> p k n", k=2)
                a = AC(lambda e: e.copy(o, bv[:, :, t, :]), tok, O[t].free)
                Otok[t].append(a)
            b.give(a)

        def retention(B, O, Otok):
            dm = [Slot() for _ in range(3)]
            dt_ = [load(dm[i].v[:, 0:768], W["ret"][:, i * 768:(i + 1) * 768], dm[i].free) for i in range(3)]
            qk = [Slot(), Slot()]
            qt = [[], []]
            src = [[(0, 0), (0, 128), (0, 256)], [(0, 384), (1, 0), (1, 128)]]
            for w in range(2):
                for f0, nf in ((0, 2), (2, 1)):
                    b = Bank()
                    PE.wait([b.free, t_con])
                    for f in range(f0, f0 + nf):
                        si, c = src[w][f]
                        for t in range(2):
                            p = PE(lambda e: e.transpose(b.v[:, (f - f0) * 256 + t * P:(f - f0) * 256 + (t + 1) * P],
                                                         B[si][0].v2[:, t, c:c + P], ident), B[si][1][t])
                    dst = qk[w].v[:, f0 * 256:(f0 + nf) * 256]
                    if w == 0:
                        a = AC(lambda e: e.copy(dst, b.v[:, 0:nf * 256]), p, qk[w].free)
                    else:
                        a = DV(lambda e: e.tensor_copy(dst, b.v[:, 0:nf * 256]), p, qk[w].free)
                    b.give(a)
                    qt[w].append(a)
            yield
            vof = lambda h, t: (B[1][0].v2[:, t, 256 + h * 128:384 + h * 128] if h < 2
                                else B[2][0].v2[:, t, (h - 2) * 128:(h - 1) * 128])
            spt = [None] * 6
            for h in range(6):
                f, p0 = h // 2, 64 * (h % 2)
                b = Bank()
                PE.wait([b.free, qt])
                q, k = qk[0].v[p0:p0 + 64, f * 256:(f + 1) * 256], qk[1].v[p0:p0 + 64, f * 256:(f + 1) * 256]
                PE(lambda e: e.matmul(b.v[:, 0:256], k[:, 0:128], q, start=True, stop=True), sig=False)
                p = PE(lambda e: e.matmul(b.v[:, 256:384], k[:, 128:256], q[:, 128:256], start=True, stop=True))
                dv = dm[h // 2].v[:, (h % 2) * 384:(h % 2) * 384 + 384]
                d = DV(lambda e: e.tensor_tensor(dv, b.v[:, 0:384], dv, ALU.mult), p, dt_)
                b.give(d)
                spt[h] = d
                if h % 2:
                    yield
            for w in range(2):
                qk[w].give((PE.sem, PE.n))

            def o_of(b, h, k):
                s = dm[h // 2].v[:, (h % 2) * 384:(h % 2) * 384 + 384]
                PE.wait([b.free, spt[h], B[1][1], B[2][1]])
                bo = lambda t: b.v[:, (2 * k + t) * P:(2 * k + t + 1) * P]
                PE(lambda e: e.matmul(bo(0), s[:, 0:128], vof(h, 0), start=True, stop=True))
                PE(lambda e: e.matmul(bo(1), s[:, 128:256], vof(h, 0), start=True, stop=False))
                PE(lambda e: e.matmul(bo(1), s[:, 256:384], vof(h, 1), start=False, stop=True))
            for hp in range(3):
                out_banks(o_of, O, Otok, hp)
                dm[hp].give((PE.sem, PE.n))
                yield

        def ret_gate(B):
            def gate(t, tok):
                s = Slot()
                for a0, n, sl, c in ((0, 512, 3, 0), (512, 256, 4, 0)):
                    g = B[sl][0].v2[:, t, c:c + n]
                    th = s.v[:, a0:a0 + n]
                    a = AC(lambda e: e.activation(th, g, ACT.Tanh, scale=0.5), B[sl][1][t], s.free)
                    d = DV(lambda e: e.scalar_tensor_tensor(th, th, 1.0, g, ALU.add, ALU.mult), a)
                ov = O[t].v[:, 0:768]
                d = DV(lambda e: e.scalar_tensor_tensor(ov, ov, 0.5, s.v[:, 0:768], ALU.mult, ALU.mult), d, tok)
                s.give(d)
                return d
            return gate

        B = []
        for i in range(3):
            run(to_slot(block(W["w_in"][0], 512 * i), xs, xtok, B))
        O = [Slot(), Slot()]
        Otok = [[], []]
        weave(chain(*(to_slot(block(W["w_in"][0], 512 * i), xs, xtok, B) for i in range(3, 5))),
              chain(retention(B, O, Otok), mem_keys(mks, kvs[1], V("mk", 1))))
        xuse[id(xs)] = [(PE.sem, PE.n)]
        qc = lambda t: B[4][0].v2[:, t, 256:512]
        vv = lambda i: (lambda m: kvs[i][0].v2[:, m, 256:512])
        kT3 = lambda i: kvs[i][0].v2[:, :, 0:256]
        weave(mem_attention(qc, B[4][1], kT3(0), vv(0), [mks[0], kvs[0][1]], O, Otok, V("mq", 0)),
              out_norm(O, Otok, 6, 128, R("ret_gn").rearrange("p (a b) -> p a b", b=128), None, ret_gate(B)))
        fin = [(PE.sem, PE.n), (DV.sem, DV.n), (AC.sem, AC.n), (PO.sem, PO.n)]
        for b_ in B:
            b_[0].give(*fin)
        kvs[0][0].give(*fin)
        otok = spread([O[0].v, O[1].v], xs, Otok)
        for t in range(2):
            O[t].give((PE.sem, PE.n))
        g1 = get_gain("ffn0")
        run(residual(W["w_out"][0], 8, xs, otok, xt))
        xuse[id(xs)] = [(PE.sem, PE.n)]

        def ffn(l, g):
            xtok = norm(lambda t: X[:, t, :], g, xs, xt)
            acc = [[Bank(), Bank()], [Bank(), Bank()]]
            wg = W["w_gate_up"][l].rearrange("(k p) (g n) -> p k g n", p=P, g=2)
            nb = FFN // 256
            act = {}

            def gate_up(b):
                s = Slot()
                box = act[b] = (s, [])

                def done(bk, tok):
                    for t in range(2):
                        w = bk[t].v
                        th = s.v2[:, t, 256:512]
                        o = s.v2[:, t, 0:256]
                        a = AC(lambda e: e.activation(th, w[:, 0:256], ACT.Tanh, scale=0.5), tok, s.free)
                        d = DV(lambda e: e.scalar_tensor_tensor(th, th, 1.0, w[:, 0:256], ALU.add, ALU.mult), a)
                        d = DV(lambda e: e.scalar_tensor_tensor(o, th, 0.5, w[:, 256:512], ALU.mult, ALU.mult), d)
                        bk[t].give(d)
                        box[1].append(d)
                return cols(lambda k: wg[:, 2 * k:2 * k + 2, :, b * 256:(b + 1) * 256], xs, xtok, done)

            def turn(b):
                s, tk = act[b]
                bk = Bank()
                PE.wait([bk.free])
                for f in range(2):
                    for t in range(2):
                        p = PE(lambda e: e.transpose(bk.v[:, f * 256 + t * P:f * 256 + (t + 1) * P],
                                                     s.v2[:, t, f * P:(f + 1) * P], ident), tk[t])
                s.give(p)
                k0 = 2 * (b % 4)
                o = lambda l_: ys[:, l_, k0:k0 + 2, :]
                a = AC(lambda e: e.copy(o(0), bk.g(2)), p, yfree[b % 4])
                d = DV(lambda e: e.tensor_tensor(o(1), bk.g(2), o(0).bitcast(F32), ALU.subtract), a)
                bk.give(d)
                return d
            yfree = [list(xuse[id(ys)]) for _ in range(4)]
            yt = {}

            def down(b):
                for tok in rows_(W["w_down"][l], [2 * b, 2 * b + 1], ys, 2 * (b % 4), yt[b], acc, b == 0, b == nb - 1):
                    pass
                yfree[b % 4] = [tok]
                return tok
            for b in range(nb):
                for k, _ in enumerate(gate_up(b)):
                    if k == 1 and b:
                        yt[b - 1] = turn(b - 1)
                if b:
                    down(b - 1)
            xuse[id(xs)] = [(PE.sem, PE.n)]
            yt[nb - 1] = turn(nb - 1)
            tok = down(nb - 1)
            xuse[id(ys)] = [tok]
            add_acc(acc, tok, xt)

        peaks.append(peak[0])
        peak[0] = 0

        def done_early():
            return SP.dma(lambda e: e.dma_start(xin(out), X[:, :, :]), s_out, 16, xt)

        peaks.append(peak[0])
        peak[0] = 0
        if stop >= 2:
            ffn(0, g1)

        def diff(B, O, Otok):
            bi = [Slot() for _ in range(3)]
            bt = [load(bi[i].v[:, 0:768], W["dif"][:, i * 768:(i + 1) * 768], bi[i].free) for i in range(3)]
            lam = small(4)
            jk = small(64)
            d = DV(lambda e: e.tensor_tensor(jk, R("lq1"), R("lk1"), ALU.mult), t_row)
            d = DV(lambda e: e.tensor_reduce(lam[:, 0:1], jk, AX.X, ALU.add), d)
            jk2 = small(64)
            d = DV(lambda e: e.tensor_tensor(jk2, R("lq2"), R("lk2"), ALU.mult), d)
            d = DV(lambda e: e.tensor_reduce(lam[:, 1:2], jk2, AX.X, ALU.add), d)
            a = AC(lambda e: e.activation(lam[:, 2:4], lam[:, 0:2], ACT.Exp), d)
            nlam = small(1)
            d = DV(lambda e: e.tensor_tensor(nlam, lam[:, 3:4], lam[:, 2:3], ALU.subtract), a)
            nl = small(1)
            tl = DV(lambda e: e.tensor_scalar(nl, nlam, -LAMBDA_INIT, None, ALU.add), d)
            wq = small(1)
            tq = DV(lambda e: e.tensor_scalar(wq, V("dq"), 0.125, None, ALU.mult), t_vec)
            qk = [Slot() for _ in range(3)]
            qt = []
            for i in range(3):
                s, tk = B[i]
                v3 = s.v.rearrange("p (a b) -> p a b", b=64)
                r, rt = group_rs(s.v, 16, 64, 1.0 / 64, EPS, tk)
                d = DV(lambda e: e.tensor_tensor(v3, v3, bc(r, 64), ALU.mult), rt)
                yield
                for f0 in (0, 2):
                    b = Bank()
                    PE.wait([b.free, d, t_con])
                    for f in range(2):
                        for t in range(2):
                            p = PE(lambda e: e.transpose(b.v[:, f * 256 + t * P:f * 256 + (t + 1) * P],
                                                         s.v2[:, t, (f0 + f) * P:(f0 + f + 1) * P], ident))
                    is_q = 4 * i + f0 < 6
                    a = AC(lambda e: e.mul(qk[i].v[:, f0 * 256:(f0 + 2) * 256], b.v, wq if is_q else V("dk")),
                           p, tq, qk[i].free)
                    b.give(a)
                    qt.append(a)
                s.give(p)
                yield
            ft = lambda n: qk[n // 4].v[:, (n % 4) * 256:(n % 4 + 1) * 256]
            vof = lambda h, t: (B[3][0].v2[:, t, h * P:(h + 1) * P] if h < 4
                                else B[4][0].v2[:, t, (h - 4) * P:(h - 3) * P])
            st = {}

            def scores(h):
                s = Slot()
                tk = []
                mx, nm, su, rc = small(4), small(4), small(4), small(4)
                sv = s.v[:, 0:768].rearrange("p (c n) -> p c n", c=2)
                part = lambda it: sv[:, :, 0:128] if it == 0 else sv[:, :, 128:384]
                bias = bi[h // 2].v[:, (h % 2) * 384:(h % 2) * 384 + 384]
                for c in range(2):
                    b = Bank()
                    PE.wait([b.free, qt])
                    q, k = ft(h)[64 * c:64 * c + 64, :], ft(6 + h)[64 * c:64 * c + 64, :]
                    PE(lambda e: e.matmul(b.v[:, 0:128], q[:, 0:128], k[:, 0:128], start=True, stop=True), sig=False)
                    p = PE(lambda e: e.matmul(b.v[:, 128:384], q[:, 128:256], k, start=True, stop=True))
                    d = DV(lambda e: e.tensor_tensor(sv[:, c, :], b.v[:, 0:384], bias, ALU.add), p, bt, s.free)
                    b.give(d)
                    tk.append(d)
                for it in range(2):
                    d = DV(lambda e: e.tensor_reduce(mx[:, 2 * it:2 * it + 2], part(it), AX.X, ALU.max), tk)
                d = DV(lambda e: e.tensor_scalar(nm, mx, -1.0, None, ALU.mult), d)
                for it in range(2):
                    for c in range(2):
                        a = AC(lambda e: e.activation(part(it)[:, c, :], part(it)[:, c, :], ACT.Exp,
                                                      bias=nm[:, 2 * it + c:2 * it + c + 1],
                                                      accum_out=su[:, 2 * it + c:2 * it + c + 1]), d)
                rc2 = small(4)
                d = DV(lambda e: e.reciprocal(rc, su), a)
                d = DV(lambda e: e.tensor_scalar(rc2, rc, nl, None, ALU.mult), d, tl)
                for it in range(2):
                    pv = part(it)
                    d2 = DV(lambda e: e.tensor_scalar(pv[:, 0, :], pv[:, 0, :], rc[:, 2 * it:2 * it + 1], None,
                                                      ALU.mult), d)
                    d2 = DV(lambda e: e.scalar_tensor_tensor(pv[:, 0, :], pv[:, 1, :], rc2[:, 2 * it + 1:2 * it + 2],
                                                             pv[:, 0, :], ALU.mult, ALU.add), d2)
                st[h] = (s, d2)

            def turn(h):
                s, d = st[h]
                b = Bank()
                PE.wait([b.free, d, t_con])
                for j, c in enumerate((0, 128, 256)):
                    p = PE(lambda e: e.transpose(b.v[:, j * P:(j + 1) * P], s.v[:, c:c + P], ident), sig=(j == 2))
                a = AC(lambda e: e.copy(s.v[:, 384:768], b.v[:, 0:384]), p)
                b.give(a)
                st[h] = (s, a)

            def o_of(b, h, k):
                s, a = st[h]
                PE.wait([b.free, a, B[3][1], B[4][1]])
                bo = lambda t: b.v[:, (2 * k + t) * P:(2 * k + t + 1) * P]
                PE(lambda e: e.matmul(bo(0), s.v[:, 384:512], vof(h, 0), start=True, stop=True))
                PE(lambda e: e.matmul(bo(1), s.v[:, 512:640], vof(h, 0), start=True, stop=False))
                p = PE(lambda e: e.matmul(bo(1), s.v[:, 640:768], vof(h, 1), start=False, stop=True))
                s.give(p)
            for h in range(6):
                scores(h)
                yield
                if h >= 2:
                    turn(h - 2)
                if h >= 4 and h % 2 == 0:
                    out_banks(o_of, O, Otok, (h - 4) // 2)
                yield
            for i in range(3):
                qk[i].give((PE.sem, PE.n))
                bi[i].give((DV.sem, DV.n))
            turn(4)
            turn(5)
            yield
            out_banks(o_of, O, Otok, 1)
            out_banks(o_of, O, Otok, 2)
            yield

        peaks.append(peak[0])
        peak[0] = 0
        if stop >= 3:
            xtok = norm(lambda t: X[:, t, :], get_gain("attn1"), xs, xt)
            B = []
            for i in range(4):
                run(to_slot(block(W["w_in"][1], 512 * i), xs, xtok, B))
            O = [Slot(), Slot()]
            Otok = [[], []]
            Otok2 = [[], []]
            df = diff(B, O, Otok)
            for _ in to_slot(block(W["w_in"][1], 2048), xs, xtok, B):
                next(df)
            xuse[id(xs)] = [(PE.sem, PE.n)]
            qc1 = lambda t: B[4][0].v2[:, t, 256:512]
            weave(mem_attention(qc1, B[4][1], kT3(1), vv(1), [mks[1], kvs[1][1]], O, Otok2, V("mq", 1)), df, 2)
            run(out_norm(O, Otok, 6, 128, bm(R("subln"), 6), 1.0 - LAMBDA_INIT))
            fin = [(PE.sem, PE.n), (DV.sem, DV.n), (AC.sem, AC.n), (PO.sem, PO.n)]
            for b_ in B[3:]:
                b_[0].give(*fin)
            kvs[1][0].give(*fin)
            otok = spread([O[0].v, O[1].v], xs, [Otok[t] + Otok2[t] for t in range(2)])
            for t in range(2):
                O[t].give((PE.sem, PE.n))
            g1 = get_gain("ffn1")
            run(residual(W["w_out"][1], 8, xs, otok, xt))
            xuse[id(xs)] = [(PE.sem, PE.n)]
        peaks.append(peak[0])
        peak[0] = 0
        if stop >= 4:
            ffn(1, g1)

        def softplus_terms(dst, src, n, tok):
            a = AC(lambda e: e.activation(dst, src, ACT.Abs), tok)
            a = AC(lambda e: e.activation(dst, dst, ACT.Exp, scale=-1.0), a)
            a = DV(lambda e: e.tensor_scalar(dst, dst, 1.0, None, ALU.add), a)
            return AC(lambda e: e.activation(dst, dst, ACT.Ln), a)

        def gdn_scalars(ga, tok, S):
            ab = ga[:, :, 0:8]
            z, sp_, g, be = (small(16).rearrange("p (t h) -> p t h", t=2) for _ in range(4))
            ea = small(8)
            a0 = AC(lambda e: e.activation(ea, R("a_log"), ACT.Exp), t_row)
            d = DV(lambda e: e.tensor_tensor(z, ab, bm(R("dt_bias"), 2), ALU.add), tok, t_row)
            l = softplus_terms(sp_, z, 16, d)
            d = DV(lambda e: e.scalar_tensor_tensor(sp_, z, 0.0, sp_, ALU.max, ALU.add), l)
            d = DV(lambda e: e.scalar_tensor_tensor(g, sp_, -1.0, bm(ea, 2), ALU.mult, ALU.mult), d, a0)
            a = AC(lambda e: e.activation(be, ga[:, :, 8:16], ACT.Exp, scale=-1.0), tok)
            db = DV(lambda e: e.tensor_scalar(be, be, 1.0, None, ALU.add), a)
            db = DV(lambda e: e.reciprocal(be, be), db)
            yield
            b = Bank()
            g2 = g.rearrange("p t h -> p (t h)")
            PE.wait([b.free, d, t_con])
            PE(lambda e: e.matmul(b.v[:, 0:16], cU, g2, start=True, stop=True), sig=False)
            PE(lambda e: e.matmul(b.v[:, 16:32], cS, g2, start=True, stop=True), sig=False)
            for c in range(2):
                p = PE(lambda e: e.matmul(b.v[:, 32 + 16 * c:48 + 16 * c],
                                          con[:, 384 + 128 * c:512 + 128 * c], g2, start=True, stop=True))
            ex = small(64)
            a = AC(lambda e: e.activation(ex, b.v[:, 0:64], ACT.Exp), p)
            b.give(a)
            yield
            S["g"], S["beta"] = g, be
            S["egc"] = ex[:, 0:16].rearrange("p (t h) -> p t h", t=2)
            S["ekd"] = ex[:, 16:32].rearrange("p (t h) -> p t h", t=2)
            S["ge"] = ex[:, 32:64].rearrange("p (c t h) -> p c t h", c=2, t=2)
            S["tok"] = [a, db, d]

        def conv_half(z, f0, box):
            s, tk = box
            y = Slot()
            yv = y.v.rearrange("p (f n) -> p f n", f=4)
            tks = []
            for fp in range(2):
                b = Bank()
                PE.wait([b.free, tk])
                for f in range(2):
                    for t in range(2):
                        p = PE(lambda e: e.transpose(b.v[:, f * 256 + t * P:f * 256 + (t + 1) * P],
                                                     s.v2[:, t, (2 * fp + f) * P:(2 * fp + f + 1) * P], ident))
                for f in range(2):
                    cw = lambda n: V("conv", (f0 + 2 * fp + f) * 4 + n)
                    o = yv[:, 2 * fp + f, :]
                    bv = b.v[:, f * 256:(f + 1) * 256]
                    d = AC(lambda e: e.mul(o, bv, cw(3)), p, y.free, t_vec)
                a = d
                for f in range(2):
                    cw = lambda n: V("conv", (f0 + 2 * fp + f) * 4 + n)
                    o = yv[:, 2 * fp + f, :]
                    bv = b.v[:, f * 256:(f + 1) * 256]
                    d = a
                    for n in (2, 1, 0):
                        sh = 3 - n
                        d = DV(lambda e: e.scalar_tensor_tensor(o[:, sh:256], bv[:, 0:256 - sh], cw(n), o[:, sh:256],
                                                                ALU.mult, ALU.add), d)
                b.give(d)
                tks.append(d)
                yield
            th = Slot()
            a = AC(lambda e: e.activation(th.v, y.v, ACT.Tanh, scale=0.5), tks, th.free)
            d = DV(lambda e: e.scalar_tensor_tensor(y.v, th.v, 1.0, y.v, ALU.add, ALU.mult), a)
            th.give(d)
            yield
            nt = []
            for t in range(2):
                b = Bank()
                PE.wait([b.free, d])
                for f in range(4):
                    p = PE(lambda e: e.transpose(b.v[:, f * P:(f + 1) * P], yv[:, f, t * P:(t + 1) * P], ident))
                a = AC(lambda e: e.copy(s.v2[:, t, :], b.v), p)
                b.give(a)
                nt.append(a)
            y.give(p)
            box[1] = nt
            yield

        def gdn(hf, box, S, res):
            for z in range(3):
                yield from conv_half(z, 8 * z + 4 * hf, box[z])
            (qs, qtk), (ks, ktk), (vs, vtk) = box
            hs = slice(4 * hf, 4 * hf + 4)
            sc = []
            for s_, tk in ((qs, qtk), (ks, ktk)):
                sc.append(group_rs(s_.v, 8, P, 0.25, EPS, tk))
            th8 = lambda a: a.rearrange("p (t h) -> p t h", t=2)
            rq, rk = th8(sc[0][0]), th8(sc[1][0])
            cq, cqd, ck, ckb, crk, ckd, cv = (small(8).rearrange("p (t h) -> p t h", t=2) for _ in range(7))
            d = DV(lambda e: e.tensor_scalar(cq, rq, 0.5 * P ** -0.5, None, ALU.mult), sc[0][1])
            tqd = DV(lambda e: e.tensor_tensor(cqd, cq, S["egc"][:, :, hs], ALU.mult), d, S["tok"])
            d = DV(lambda e: e.tensor_scalar(ck, rk, 0.5, None, ALU.mult), sc[1][1])
            d2 = DV(lambda e: e.tensor_tensor(ckb, ck, S["beta"][:, :, hs], ALU.mult), d)
            DV(lambda e: e.tensor_tensor(ckd, ck, S["ekd"][:, :, hs], ALU.mult), d)
            DV(lambda e: e.tensor_tensor(crk, ckb, S["egc"][:, :, hs], ALU.mult), d2)
            tcf = DV(lambda e: e.tensor_scalar(cv, S["beta"][:, :, hs], 0.5, None, ALU.mult), S["tok"])
            h4 = lambda a: a.rearrange("p (h n) -> p h n", h=4)
            kT = Slot()
            lq = [Slot(), Slot()]
            qd = Slot()
            rkS = Slot()
            rt_ = PO(lambda e: e.tensor_tensor(rkS.v.rearrange("p (a n) -> p a n", n=P),
                                               ks.v.rearrange("p (a n) -> p a n", n=P),
                                               bc(crk.rearrange("p t h -> p (t h)"), P), ALU.mult),
                     tcf, ktk, rkS.free)
            kTt, lqt, qdt = [], [[], []], []
            for t in range(2):
                for c, src, stk, dst, fr, lst in (
                        (ck, ks, ktk, h4(kT.v2[:, t, :]), kT.free, kTt),
                        (ckb, ks, ktk, lq[t].v.rearrange("p (h l n) -> p h l n", h=4, l=2)[:, :, 0, :], lq[t].free, lqt[t]),
                        (cq, qs, qtk, lq[t].v.rearrange("p (h l n) -> p h l n", h=4, l=2)[:, :, 1, :], lq[t].free, lqt[t]),
                        (cqd, qs, qtk, h4(qd.v2[:, t, :]), qd.free, qdt)):
                    tmp = Slot()
                    m = DV(lambda e: e.tensor_tensor(h4(tmp.v[:, 0:512]), h4(src.v2[:, t, :]), bc(c[:, t, :], P),
                                                     ALU.mult), tcf, stk, tmp.free, tqd)
                    b = Bank()
                    PE.wait([b.free, m])
                    for h in range(4):
                        p = PE(lambda e: e.transpose(b.v[:, h * P:(h + 1) * P], tmp.v[:, h * P:(h + 1) * P], ident))
                    a = AC(lambda e: e.copy(dst, b.g(4)), p, fr)
                    b.give(a)
                    tmp.give(p)
                    lst.append(a)
                yield
            k3 = ks.v.rearrange("p (a n) -> p a n", n=P)
            kdt = DV(lambda e: e.tensor_tensor(k3, k3, bc(ckd.rearrange("p t h -> p (t h)"), P), ALU.mult), rt_, kTt, lqt)
            v3 = vs.v.rearrange("p (a n) -> p a n", n=P)
            rvt = PO(lambda e: e.tensor_tensor(v3, v3, bc(cv.rearrange("p t h -> p (t h)"), P), ALU.mult), tcf, vtk)
            dec = Slot()
            gU = Slot()
            dt_ = []
            for t in range(2):
                gv = h4(gU.v2[:, t, :])
                m = PO(lambda e: e.tensor_tensor(gv, bm(cU, 4), bc(S["g"][:, t, hs], P), ALU.mult), S["tok"], gU.free)
                b = Bank()
                p = PE(lambda e: e.matmul(b.v, cS, gU.v2[:, t, :], start=True, stop=True), m, b.free)
                dv = dec.v2[:, t, :]
                a = AC(lambda e: e.activation(dv, b.v, ACT.Exp), p, dec.free)
                b.give(a)
                dt_.append(PO(lambda e: e.tensor_tensor(h4(dv), h4(dv), bm(cU, 4), ALU.mult), a))
            gU.give(p)
            yield
            la = [Slot(), Slot()]
            lat = [[], []]
            for t in range(2):
                for hp in range(2):
                    b = Bank()
                    PE.wait([b.free, kTt[t], lqt[t]])
                    for k in range(2):
                        h = 2 * hp + k
                        p = PE(lambda e: e.matmul(b.v[:, k * 256:(k + 1) * 256], kT.v2[:, t, h * P:(h + 1) * P],
                                                  lq[t].v[:, h * 256:(h + 1) * 256], start=True, stop=True))
                    o = la[t].v[:, hp * 512:(hp + 1) * 512].rearrange("p (h l n) -> p h l n", h=2, l=2)
                    bv = b.v.rearrange("p (h l n) -> p h l n", h=2, l=2)
                    dd = h4(dec.v2[:, t, :])[:, 2 * hp:2 * hp + 2, :]
                    for l in range(2):
                        d = DV(lambda e: e.tensor_tensor(o[:, :, l, :], bv[:, :, l, :], dd, ALU.mult), p, dt_[t], la[t].free)
                    b.give(d)
                    lat[t].append(d)
                lq[t].give(p)
                yield
            kT.give((PE.sem, PE.n))
            dec.give((DV.sem, DV.n))
            M, N, Tt, Cm = Slot(), Slot(), Slot(), Slot()
            LT = lambda t: la[t].v.rearrange("p (h l n) -> p h l n", h=4, l=2)[:, :, 0, :]
            AT = lambda t, h: la[t].v[:, h * 256 + P:h * 256 + 2 * P]
            mt, nt_, ct = [None, None], [None, None], [None, None]
            idb = bm(ident, 4)
            cfree = [list(Cm.free), list(Cm.free)]
            tfree = [list(Tt.free), list(Tt.free)]
            for lv in range(6):
                mask = bm(con[:, 640 + P * lv:768 + P * lv], 4)
                for t in range(2):
                    cv_ = h4(Cm.v2[:, t, :])
                    ct[t] = PO(lambda e: e.tensor_tensor(cv_, LT(t), mask, ALU.mult), lat[t], cfree[t])
                for t in range(2):
                    b = Bank()
                    PE.wait([b.free, ct[t], mt[t], nt_[t]])
                    for h in range(4):
                        hh = slice(h * P, (h + 1) * P)
                        if lv == 0:
                            p = PE(lambda e: e.transpose(b.v[:, hh], Cm.v2[:, t, hh], ident))
                        else:
                            p = PE(lambda e: e.matmul(b.v[:, hh], Cm.v2[:, t, hh], M.v2[:, t, hh], start=True, stop=True))
                    if lv == 0:
                        mt[t] = DV(lambda e: e.scalar_tensor_tensor(h4(M.v2[:, t, :]), b.g(4), -1.0, idb,
                                                                    ALU.mult, ALU.add), p, M.free)
                        b.give(mt[t])
                        nt_[t] = DV(lambda e: e.scalar_tensor_tensor(h4(N.v2[:, t, :]), h4(Cm.v2[:, t, :]), -1.0, idb,
                                                                     ALU.mult, ALU.add), ct[t], N.free)
                        cfree[t] = [nt_[t], p]
                        continue
                    cfree[t] = [p]
                    tt = AC(lambda e: e.copy(Tt.v2[:, t, :], b.v), p, tfree[t])
                    b.give(tt)
                    tfree[t] = tt
                yield
                if lv == 0:
                    continue
                for t in range(2):
                    bM = Bank() if lv < 5 else None
                    bN = Bank()
                    PE.wait([tfree[t], bN.free, bM.free if bM else None])
                    if bM:
                        for h in range(4):
                            hh = slice(h * P, (h + 1) * P)
                            p1 = PE(lambda e: e.matmul(bM.v[:, hh], N.v2[:, t, hh], Tt.v2[:, t, hh], start=True, stop=True))
                    for h in range(4):
                        hh = slice(h * P, (h + 1) * P)
                        p = PE(lambda e: e.matmul(bN.v[:, hh], Tt.v2[:, t, hh], N.v2[:, t, hh], start=True, stop=True))
                    if bM:
                        mt[t] = DV(lambda e: e.scalar_tensor_tensor(M.v2[:, t, :], bM.v, -1.0, M.v2[:, t, :],
                                                                    ALU.mult, ALU.add), p1)
                        bM.give(mt[t])
                    nt_[t] = DV(lambda e: e.scalar_tensor_tensor(N.v2[:, t, :], bN.v, -1.0, N.v2[:, t, :],
                                                                 ALU.mult, ALU.add), p)
                    bN.give(nt_[t])
                    tfree[t] = [p]
                yield
            last = [(PE.sem, PE.n), (DV.sem, DV.n), (PO.sem, PO.n)]
            M.give(*last)
            Tt.give(*last)
            Cm.give(*last)
            us, wT = Slot(), Slot()
            ut, wt = [], []
            for t in range(2):
                b = Bank()
                PE.wait([b.free, nt_[t], rvt])
                for h in range(4):
                    hh = slice(h * P, (h + 1) * P)
                    p = PE(lambda e: e.matmul(b.v[:, hh], N.v2[:, t, hh], vs.v2[:, t, hh], start=True, stop=True))
                a = AC(lambda e: e.copy(us.v2[:, t, :], b.v), p, us.free)
                b.give(a)
                ut.append(a)
                b = Bank()
                PE.wait([b.free, rt_])
                for h in range(4):
                    hh = slice(h * P, (h + 1) * P)
                    p = PE(lambda e: e.matmul(b.v[:, hh], rkS.v2[:, t, hh], N.v2[:, t, hh], start=True, stop=True))
                a = AC(lambda e: e.copy(wT.v2[:, t, :], b.v), p, wT.free)
                b.give(a)
                wt.append(a)
            N.give(p)
            rkS.give(p)
            yield
            St = Slot()
            sv = St.v[:, 0:512]
            stok = None
            ot = []
            oslot = Slot()
            for c in range(4):
                t, p0 = c // 2, 64 * (c % 2)
                rows = slice(p0, p0 + 64)
                dl = us.v2[rows, t, :]
                dtok = ut[t]
                if c:
                    b = Bank()
                    PE.wait([b.free, wt[t], stok])
                    for h in range(4):
                        p = PE(lambda e: e.matmul(b.v[rows, h * P:(h + 1) * P], wT.v2[:, t, h * P + p0:h * P + p0 + 64],
                                                  sv[:, h * P:(h + 1) * P], start=True, stop=True))
                    dtok = DV(lambda e: e.scalar_tensor_tensor(dl, b.v[rows, :], -1.0, dl, ALU.mult, ALU.add), p, ut[t])
                    b.give(dtok)
                    yield
                if c < 3:
                    b = Bank()
                    PE.wait([b.free, dtok, kdt])
                    for h in range(4):
                        hh = slice(h * P, (h + 1) * P)
                        p = PE(lambda e: e.matmul(b.v[:, hh], ks.v2[rows, t, hh], us.v2[rows, t, hh], start=True, stop=True))
                kb_, kp = b, p
                b = Bank()
                PE.wait([b.free, dtok, qdt[t], lat[t], stok])
                for h in range(4):
                    hh = slice(h * P, (h + 1) * P)
                    if c:
                        PE(lambda e: e.matmul(b.v[rows, hh], qd.v2[:, t, h * P + p0:h * P + p0 + 64], sv[:, hh],
                                              start=True, stop=False), sig=False)
                    p = PE(lambda e: e.matmul(b.v[rows, hh], AT(t, h)[rows, p0:p0 + 64], us.v2[rows, t, hh],
                                              start=(c == 0), stop=True))
                a = AC(lambda e: e.copy(oslot.v2[rows, t, :], b.v[rows, :]), p, oslot.free)
                b.give(a)
                ot.append(a)
                if c == 0:
                    stok = DV(lambda e: e.tensor_copy(sv, kb_.v), kp, St.free)
                    kb_.give(stok)
                elif c < 3:
                    m = PO(lambda e: e.tensor_tensor(h4(sv), h4(sv), bc(S["ge"][:, c % 2, t, hs], P), ALU.mult), p, stok)
                    stok = DV(lambda e: e.tensor_tensor(sv, kb_.v, sv, ALU.add), kp, m)
                    kb_.give(stok)
                yield
            end = [(PE.sem, PE.n), (DV.sem, DV.n), (AC.sem, AC.n), (PO.sem, PO.n)]
            for s_ in (qs, ks, vs, us, wT, St, qd, la[0], la[1]):
                s_.give(*end)
            res.append((oslot, ot))
            yield

        def gla(box, ga, gtok, res):
            (qs, qtk), (ks, ktk) = box[0], box[1]
            tg = load(gl2[:, :], W["gate2"])
            reset = Slot()
            m = PO(lambda e: e.memset(reset.v, 1.0), reset.free)
            rv = reset.v.rearrange("p (a n) -> p a n", n=64)
            m = PO(lambda e: e.memset(rv[:, :, 0:1], 0.0), m)
            b = Bank()
            PE.wait([b.free, gtok, t_con])
            for t in range(2):
                p = PE(lambda e: e.transpose(b.v[0:16, t * P:(t + 1) * P], ga[:, t, 16:32], ident))
            lg = Slot()
            a = AC(lambda e: e.copy(lg.v[0:16, 0:256], b.v[0:16, 0:256]), p, lg.free)
            b.give(a)
            yield
            z = Slot()
            zt = []
            for hp in range(2):
                b = Bank()
                PE.wait([b.free, a, tg])
                for k in range(2):
                    h = 2 * hp + k
                    p = PE(lambda e: e.matmul(b.v[:, k * 256:(k + 1) * 256], gl2[:, h * P:(h + 1) * P],
                                              lg.v[0:16, 0:256], start=True, stop=True))
                for k in range(2):
                    h = 2 * hp + k
                    d = DV(lambda e: e.tensor_scalar(z.v[:, h * 256:(h + 1) * 256], b.v[:, k * 256:(k + 1) * 256],
                                                     V("b_gate", h), None, ALU.add), p, z.free, t_vec)
                b.give(d)
                zt.append(d)
            lg.give(p)
            yield
            l = Slot()
            d = AC(lambda e: e.activation(l.v, z.v, ACT.Abs), zt, l.free)
            d = AC(lambda e: e.activation(l.v, l.v, ACT.Exp, scale=-1.0), d)
            d = DV(lambda e: e.tensor_scalar(l.v, l.v, 1.0, None, ALU.add), d)
            d = AC(lambda e: e.activation(l.v, l.v, ACT.Ln), d)
            d = DV(lambda e: e.scalar_tensor_tensor(l.v, z.v, 0.0, l.v, ALU.min, ALU.subtract), d)
            bcum = z
            d = DV(lambda e: e.tensor_tensor_scan(bcum.v, reset.v, l.v, 0.0, ALU.mult, ALU.add), d, m)
            reset.give(d)
            yield
            b64 = bcum.v.rearrange("p (a n) -> p a n", n=64)
            e4, e1, e2 = Slot(), l, Slot()
            v64 = lambda s: s.v.rearrange("p (a n) -> p a n", n=64)
            dr = DV(lambda e: e.tensor_tensor(v64(e1), b64, b64[:, :, 32:33].to_broadcast([P, 16, 64]), ALU.subtract), d)
            dl = DV(lambda e: e.tensor_tensor(v64(e4), b64[:, :, 63:64].to_broadcast([P, 16, 64]), b64, ALU.subtract),
                    d, e4.free)
            gend = small(16)
            tau = 1.0 / 16.0
            ag = AC(lambda e: e.activation(gend.unsqueeze(2), b64[:, :, 63:64], ACT.Exp, scale=tau), d)
            a2 = AC(lambda e: e.activation(e2.v, e1.v, ACT.Exp, scale=-tau), dr, e2.free)
            a1 = AC(lambda e: e.activation(e1.v, e1.v, ACT.Exp, scale=tau), a2)
            a4 = AC(lambda e: e.activation(e4.v, e4.v, ACT.Exp, scale=tau), dl)
            a3 = AC(lambda e: e.activation(bcum.v, bcum.v, ACT.Exp, scale=tau), dl, ag)
            qT, kT = Slot(), Slot()
            tt = [[], []]
            for w, (s_, tk, dst, sc_) in enumerate(((qs, qtk, qT, P ** -0.5), (ks, ktk, kT, 1.0))):
                for hp in range(2):
                    b = Bank()
                    PE.wait([b.free, tk])
                    for k in range(2):
                        for t in range(2):
                            p = PE(lambda e: e.transpose(b.v[:, k * 256 + t * P:k * 256 + (t + 1) * P],
                                                         s_.v2[:, t, (2 * hp + k) * P:(2 * hp + k + 1) * P], ident))
                    a = AC(lambda e: e.mul(dst.v[:, hp * 512:(hp + 1) * 512], b.v, sc_), p, dst.free)
                    b.give(a)
                    tt[w].append(a)
            qs.give(p)
            ks.give(p)
            yield
            q1 = DV(lambda e: e.tensor_tensor(e1.v, e1.v, qT.v, ALU.mult), a1, tt[0])
            k2 = DV(lambda e: e.tensor_tensor(e2.v, e2.v, kT.v, ALU.mult), a2, tt[1])
            q3 = PO(lambda e: e.tensor_tensor(bcum.v, bcum.v, qT.v, ALU.mult), a3, tt[0])
            k4 = PO(lambda e: e.tensor_tensor(e4.v, e4.v, kT.v, ALU.mult), a4, tt[1])
            yield
            qT.give(q1, q3)
            kT.give(k2, k4)
            kd = Slot()
            kdt = []
            for t in range(2):
                b = Bank()
                PE.wait([b.free, k4])
                for h in range(4):
                    p = PE(lambda e: e.transpose(b.v[:, h * P:(h + 1) * P], e4.v[:, h * 256 + t * P:h * 256 + (t + 1) * P], ident))
                a = AC(lambda e: e.copy(kd.v2[:, t, :], b.v), p, kd.free)
                b.give(a)
                kdt.append(a)
            e4.give(p)
            at = Slot()
            att = []
            for t in range(2):
                b = Bank()
                PE.wait([b.free, q1, k2])
                for h in range(4):
                    cc = slice(h * 256 + t * P, h * 256 + (t + 1) * P)
                    p = PE(lambda e: e.matmul(b.v[:, h * P:(h + 1) * P], e2.v[:, cc], e1.v[:, cc], start=True, stop=True))
                a = AC(lambda e: e.copy(at.v2[:, t, :], b.v), p, at.free)
                b.give(a)
                av = at.v2[:, t, :].rearrange("p (h n) -> p h n", h=4)
                att.append(PO(lambda e: e.affine_select(out=av, in_=av, pattern=[[0, 4], [1, P]], compare_op=ALU.is_ge,
                                                        fill=0.0, base=0, channel_multiplier=-1), a))
            e1.give(p)
            e2.give(p)
            yield
            vsl = lambda h: box[2 + h // 2][0].v2[:, :, (h % 2) * 256:(h % 2 + 1) * 256]
            vtok = [box[2][1], box[3][1]]
            St = Slot()
            stok = None
            oo = [Slot(), Slot()]
            ot = [[], []]
            for c in range(4):
                t, p0 = c // 2, 64 * (c % 2)
                rows = slice(p0, p0 + 64)
                kb_ = []
                if c < 3:
                    for hp in range(2):
                        b = Bank()
                        PE.wait([b.free, kdt, vtok])
                        for k in range(2):
                            h = 2 * hp + k
                            p = PE(lambda e: e.matmul(b.v[:, k * 256:(k + 1) * 256], kd.v2[rows, t, h * P:(h + 1) * P],
                                                      vsl(h)[rows, t, :], start=True, stop=True))
                        kb_.append((b, p))
                for hp in range(2):
                    b = Bank()
                    PE.wait([b.free, att[t], q3, stok, vtok])
                    for k in range(2):
                        h = 2 * hp + k
                        bo = b.v[rows, k * 256:(k + 1) * 256]
                        if c:
                            PE(lambda e: e.matmul(bo, bcum.v[:, h * 256 + c * 64:h * 256 + c * 64 + 64],
                                                  St.v[:, h * 256:(h + 1) * 256], start=True, stop=False), sig=False)
                        p = PE(lambda e: e.matmul(bo, at.v2[rows, t, h * P + p0:h * P + p0 + 64], vsl(h)[rows, t, :],
                                                  start=(c == 0), stop=True))
                    a = AC(lambda e: e.copy(oo[t].v[rows, hp * 512:(hp + 1) * 512], b.v[rows, :]), p, oo[t].free)
                    b.give(a)
                    ot[t].append(a)
                s4 = St.v.rearrange("p (h n) -> p h n", h=4)
                if 0 < c < 3:
                    gv = gend.rearrange("p (h c) -> p h c", c=4)[:, :, c]
                    m = PO(lambda e: e.tensor_tensor(s4, s4, bc(gv, 256), ALU.mult), p, stok)
                nst = []
                for hp, (b, kp) in enumerate(kb_):
                    s2 = St.v[:, hp * 512:(hp + 1) * 512]
                    if c == 0:
                        d = DV(lambda e: e.tensor_copy(s2, b.v), kp, St.free)
                    else:
                        d = DV(lambda e: e.tensor_tensor(s2, b.v, s2, ALU.add), kp, m)
                    b.give(d)
                    nst.append(d)
                stok = nst
                yield
            end = [(PE.sem, PE.n), (DV.sem, DV.n), (AC.sem, AC.n), (PO.sem, PO.n)]
            for s_ in (bcum, kd, at, St, box[2][0], box[3][0]):
                s_.give(*end)
            res.append((oo, ot))

        def gate_in(B2, mulc=None):
            s, tk = B2
            th = Slot()
            a = AC(lambda e: e.activation(th.v, s.v, ACT.Tanh, scale=0.5), tk, th.free)
            d = DV(lambda e: e.scalar_tensor_tensor(s.v, th.v, 1.0, s.v, ALU.add, ALU.mult), a)
            th.give(d)
            return d

        peaks.append(peak[0])
        peak[0] = 0
        if stop >= 5:
            xtok = norm(lambda t: X[:, t, :], get_gain("mix2"), xs, xt)
            W2 = W["w_in_2"]
            ga = Slot()
            gav = ga.v[:, 0:64].rearrange("p (t n) -> p t n", t=2)
            w3 = W2.rearrange("(k p) n -> p k n", p=P)
            t1 = load(sraw[:, :, 0:16], w3[:, :, 4096:4112])
            t2 = load(sraw[:, :, 16:32], w3[:, :, 7184:7200])
            a = AC(lambda e: e.copy(sspl[:, 0], sraw[:, :, :]), t1, t2)
            d = DV(lambda e: e.tensor_tensor(sspl[:, 1], sraw[:, :, :], sspl[:, 0].bitcast(F32), ALU.subtract), a)
            b = Bank()
            PE.wait([b.free, d, xtok])
            for t in range(2):
                for k in range(8):
                    for n, (l, m) in enumerate(((0, 0), (0, 1), (1, 0))):
                        p = PE(lambda e: e.matmul(b.v[:, t * 32:(t + 1) * 32], xs[:, l, k, t * P:(t + 1) * P],
                                                  sspl[:, m, k, :], start=(k == 0 and n == 0), stop=(k == 7 and n == 2)))
            gtok = AC(lambda e: e.copy(gav, b.v[:, 0:64].rearrange("p (t n) -> p t n", t=2)), p, ga.free)
            b.give(gtok)
            S = {}
            BA, BB = [], []
            ho = []
            sc_g = gdn_scalars(gav, gtok, S)
            weave(chain(*(to_slot(block(W2, c), xs, xtok, BA) for c in (0, 1024, 2048))), sc_g)
            BA = [list(x_) for x_ in BA]
            GL = []
            gA = gdn(0, BA, S, ho)
            weave(chain(*(to_slot(block(W2, c), xs, xtok, BB) for c in (512, 1536, 2560)),
                        *(to_slot(block(W2, c), xs, xtok, GL) for c in (4112, 4624))), gA)
            BB = [list(x_) for x_ in BB]
            Z = []
            gB = gdn(1, BB, S, ho)
            weave(chain(*(to_slot(block(W2, c), xs, xtok, GL) for c in (5136, 5648)),
                        *(to_slot(block(W2, c), xs, xtok, Z) for c in (3072, 3584))), gB)
            go = []

            def out_gdn():
                for hf in range(2):
                    s, tk = ho[hf]
                    r, rt = group_rs(s.v, 8, P, 1.0 / P, EPS, tk, 0.5)
                    d = gate_in(Z[hf])
                    o8 = s.v.rearrange("p (a n) -> p a n", n=P)
                    d1 = DV(lambda e: e.tensor_tensor(o8, o8, bc(r, P), ALU.mult), rt)
                    d1 = PO(lambda e: e.tensor_tensor(o8, o8, bm(R("gdn_g"), 8), ALU.mult), d1, t_row)
                    d1 = DV(lambda e: e.tensor_tensor(s.v, s.v, Z[hf][0].v, ALU.mult), d1, d)
                    Z[hf][0].give(d1)
                    ya.append(d1)
                    yield
            ya = []
            weave(chain(*(to_slot(block(W2, c), xs, xtok, Z) for c in (6160, 6672))),
                  chain(out_gdn()))
            yat = []
            for t in range(2):
                for hf in range(2):
                    yat.append(halves(ho[hf][0].v2[:, t, :], ys, 4 * hf, 4, t, ya[hf]))
            xuse[id(ys)] = []
            for hf in range(2):
                ho[hf][0].give((PE.sem, PE.n))
            G = []
            weave(chain(*(to_slot(block(W2, c), xs, xtok, G) for c in (7200, 7712, 8224, 8736))),
                  gla(GL, gav, gtok, go))
            xuse[id(xs)] = [(PE.sem, PE.n)]
            ga.give((DV.sem, DV.n), (PE.sem, PE.n))

            def merged(w, xin_, xtok_, gs, prev, box):
                acc = [[Bank(), Bank()], [Bank(), Bank()]]
                for tok in rows_(w, range(8), xin_, 0, xtok_, acc, True, True):
                    yield
                for j in range(2):
                    s, tk = gs[j]
                    a = AC(lambda e: e.activation(s.v, s.v, ACT.Tanh, scale=0.5), tk)
                    for t in range(2):
                        v = s.v2[:, t, :]
                        d = DV(lambda e: e.scalar_tensor_tensor(v, v, 1.0, acc[t][j].v, ALU.add, ALU.mult), a, tok)
                        acc[t][j].give(d)
                    if prev is not None:
                        d = DV(lambda e: e.tensor_tensor(s.v, s.v, prev[j][0].v, ALU.add), d, prev[j][1])
                        d = DV(lambda e: e.tensor_scalar(s.v, s.v, 0.5, None, ALU.mult), d)
                        prev[j][0].give(d)
                    box.append((s, d))

            (oo, ot) = go[0]

            def out_gla():
                for t in range(2):
                    s = oo[t]
                    r, rt = group_rs(s.v, 4, 256, 1.0 / 256, EPS, ot[t], 0.5)
                    o4 = s.v.rearrange("p (a n) -> p a n", n=256)
                    d1 = DV(lambda e: e.tensor_tensor(o4, o4, bc(r, 256), ALU.mult), rt)
                    d1 = PO(lambda e: e.tensor_tensor(o4, o4, bm(R("gla_g"), 4), ALU.mult), d1, t_row)
                    for hf in range(2):
                        if t == 0:
                            lr.append(gate_in(Z[2 + hf]))
                        sv = s.v[:, hf * 512:(hf + 1) * 512]
                        zv = Z[2 + hf][0].v2[:, t, :]
                        d2 = DV(lambda e: e.tensor_tensor(sv, sv, zv, ALU.mult), d1, lr[hf])
                    yb.append(d2)
                    yield
                for hf in range(2):
                    Z[2 + hf][0].give(d2)
            lr, yb = [], []
            m1, m2 = [], []
            weave(merged(W["w_branch_gdn"], ys, yat, G[0:2], None, m1), out_gla())
            xuse[id(ys)] = [(PE.sem, PE.n)]
            ybt = spread([oo[0].v, oo[1].v], xs, yb)
            for t in range(2):
                oo[t].give((PE.sem, PE.n))
            run(merged(W["w_branch_gla"], xs, ybt, G[2:4], m1, m2))
            mt_ = []
            for t in range(2):
                for j in range(2):
                    mt_.append(halves(m2[j][0].v2[:, t, :], ys, 4 * j, 4, t, m2[j][1]))
            for j in range(2):
                m2[j][0].give((PE.sem, PE.n))
            xuse[id(xs)] = [(PE.sem, PE.n)]
            xuse[id(ys)] = []
            mem_s = [Slot(), Slot()]
            m_tok = [load(mem_s[t].v, W["mem2"][0, t * P:(t + 1) * P, :], mem_s[t].free) for t in range(2)]
            run(residual(W["w_out_2"], 8, ys, mt_, xt))
            xuse[id(ys)] = [(PE.sem, PE.n)]

        peaks.append(peak[0])
        peak[0] = 0
        if stop >= 6:
            mtok = norm(lambda t: mem_s[t].v, get_gain("mem2"), ys, m_tok)
            for t in range(2):
                mem_s[t].give((DV.sem, DV.n), (PE.sem, PE.n))
            gx = get_gain("xattn")
            K, Vv, Q = [], [], []
            xn = []

            def later():
                xn.extend(norm(lambda t: X[:, t, :], gx, xs, xt))
                yield
            weave(chain(*(to_slot(block(W["xattn_wk"], c), ys, mtok, K) for c in (0, 512))), later())
            kT = [Slot(), Slot()]

            def turn_feat(B_, dst, scale, toks):
                for i in range(2):
                    s, tk = B_[i]
                    for fp in range(2):
                        b = Bank()
                        PE.wait([b.free, tk])
                        for f in range(2):
                            for t in range(2):
                                p = PE(lambda e: e.transpose(b.v[:, f * 256 + t * P:f * 256 + (t + 1) * P],
                                                             s.v2[:, t, (2 * fp + f) * P:(2 * fp + f + 1) * P], ident))
                        a = AC(lambda e: e.mul(dst[i].v[:, fp * 512:(fp + 1) * 512], b.v, scale), p, dst[i].free)
                        b.give(a)
                        toks.append(a)
                    s.give(p)
                    yield
            ktk, qtk = [], []
            weave(chain(*(to_slot(block(W["xattn_wv"], c), ys, mtok, Vv) for c in (0, 512))),
                  turn_feat(K, kT, 1.0, ktk))
            xuse[id(ys)] = [(PE.sem, PE.n)]
            run(chain(*(to_slot(block(W["xattn_wq"], c), xs, xn, Q) for c in (0, 512))))
            xuse[id(xs)] = [(PE.sem, PE.n)]
            qT = [Slot(), Slot()]
            run(turn_feat(Q, qT, 1.0 / 16.0, qtk))
            gm = get_gain("mlp")
            ftT = lambda s, f: s[f // 4].v[:, (f % 4) * 256:(f % 4 + 1) * 256]
            wTs = []

            def xat(t):
                sc, st_ = [], []
                for hp in range(2):
                    b = Bank()
                    PE.wait([b.free, qtk, ktk])
                    for k in range(2):
                        h = 2 * hp + k
                        for f in range(2):
                            p = PE(lambda e: e.matmul(b.v[:, k * 256:(k + 1) * 256],
                                                      ftT(qT, 2 * h + f)[:, t * P:(t + 1) * P], ftT(kT, 2 * h + f),
                                                      start=(f == 0), stop=(f == 1)))
                    sc.append(b)
                    st_.append(p)
                w, wtok = softmax_mem(t, sc, st_, 256)
                yield
                wT = Slot()
                tt = transposed8(w.v, wtok, wT.v, wT.free)
                w.give((PE.sem, PE.n))
                wTs.append((wT, tt))
                yield
            g0, g1_ = xat(0), xat(1)
            next(g0)
            next(g1_)
            run(g0)
            run(g1_)
            oxt = []
            for h in range(4):
                b = Bank()
                vs_ = Vv[h // 2]
                PE.wait([b.free, wTs[0][1], wTs[1][1], vs_[1]])
                for f in range(2):
                    for t in range(2):
                        for m in range(2):
                            p = PE(lambda e: e.matmul(b.v[:, f * 256 + t * P:f * 256 + (t + 1) * P],
                                                      vs_[0].v2[:, m, (h % 2) * 256 + f * P:(h % 2) * 256 + (f + 1) * P],
                                                      wTs[t][0].v[:, (2 * h + m) * P:(2 * h + m + 1) * P],
                                                      start=(m == 0), stop=(m == 1)))
                o = lambda l_: ys[:, l_, 2 * h:2 * h + 2, :]
                a = AC(lambda e: e.copy(o(0), b.g(2)), p, *xuse[id(ys)])
                d = DV(lambda e: e.tensor_tensor(o(1), b.g(2), o(0).bitcast(F32), ALU.subtract), a)
                b.give(d)
                oxt.append(d)
            for s_ in (qT + kT + [Vv[0][0], Vv[1][0], wTs[0][0], wTs[1][0]]):
                s_.give((PE.sem, PE.n))
            run(residual(W["xattn_wo"], 8, ys, oxt, xt))
            xuse[id(ys)] = [(PE.sem, PE.n)]

        peaks.append(peak[0])
        peak[0] = 0
        if stop >= 7:
            xtok = norm(lambda t: X[:, t, :], gm, xs, xt)
            gf = get_gain("final")
            acc = [[Bank(), Bank()], [Bank(), Bank()]]
            act = {}

            def up(b):
                s = Slot()
                box = act[b] = (s, [])

                def done(bk, tok):
                    for t in range(2):
                        v = s.v2[:, t, :]
                        a = AC(lambda e: e.activation(v, bk[t].v, ACT.Relu), tok, s.free)
                        bk[t].give(a)
                        box[1].append(PO(lambda e: e.tensor_tensor(v, v, v, ALU.mult), a))
                return cols(block(W["mlp_w1"], 512 * b), xs, xtok, done)
            yt = {}
            yfree = [list(xuse[id(ys)]), list(xuse[id(ys)])]

            def turn_m(b, t):
                s, tk = act[b]
                bk = Bank()
                PE.wait([bk.free, tk[t]])
                for f in range(4):
                    p = PE(lambda e: e.transpose(bk.v[:, f * P:(f + 1) * P], s.v2[:, t, f * P:(f + 1) * P], ident))
                k0 = 4 * (b % 2)
                o = lambda l_: ys[:, l_, k0:k0 + 4, t * P:(t + 1) * P]
                a = AC(lambda e: e.copy(o(0), bk.g(4)), p, yfree[b % 2])
                d = DV(lambda e: e.tensor_tensor(o(1), bk.g(4), o(0).bitcast(F32), ALU.subtract), a)
                bk.give(d)
                if t == 1:
                    s.give(p)
                yt.setdefault(b, []).append(d)

            def down_m(b):
                for tok in rows_(W["mlp_w2"], range(4 * b, 4 * b + 4), ys, 4 * (b % 2), yt[b], acc, b == 0, b == 7):
                    pass
                yfree[b % 2] = [tok]
                return tok
            for b in range(8):
                for k, _ in enumerate(up(b)):
                    if k in (1, 2) and b:
                        turn_m(b - 1, k - 1)
                if b:
                    down_m(b - 1)
            turn_m(7, 0)
            turn_m(7, 1)
            tok = down_m(7)
            add_acc(acc, tok, xt)
            gi, gt = gf
            for t in range(2):
                s = Slot()
                ss = small(1)
                a = AC(lambda e: e.activation(s.v, X[:, t, :], ACT.Square, accum_out=ss), xt[t], s.free)
                r, rt = rsqrt(ss, 1, 1.0 / D, EPS, a)
                d = DV(lambda e: e.scalar_tensor_tensor(s.v, X[:, t, :], r, gain[:, gi, :], ALU.mult, ALU.mult), rt, gt)
                SP.dma(lambda e: e.dma_start(out[0, t * P:(t + 1) * P, :], s.v), s_out, 16 * (t + 1), d)
            SP.wait([(s_out, 32)])
        else:
            done_early()
            SP.wait([(s_out, 16)] + [(s, 16) for s in s_ld[:ld[0]]])
        return order if dry else (peaks, sm[0], ld[0], len(order))


def lay_out(inputs):
    a = {k: np.asarray(v) for k, v in inputs.items()}
    f = np.float32
    con, ret, dif = shape_constants()
    arr = {
        "x": a["x"], "mem": a["mem"], "mem2": a["mem_2"], "w_in": a["w_in"], "w_out": a["w_out"],
        "w_mem_kv": a["w_mem_kv"], "w_gate_up": a["w_gate_up"], "w_down": a["w_down"],
        "w_in_2": a["w_in_2"][0], "w_branch_gdn": a["w_branch_gdn_2"][0], "w_branch_gla": a["w_branch_gla_2"][0],
        "w_out_2": a["w_out_2"][0], "xattn_wq": a["xattn_wq_2"][0], "xattn_wk": a["xattn_wk_2"][0],
        "xattn_wv": a["xattn_wv_2"][0], "xattn_wo": a["xattn_wo_2"][0], "mlp_w1": a["mlp_w1_2"][0],
        "mlp_w2": a["mlp_w2_2"][0], "gate2": a["gla_w_gate2_2"][0],
        "con": con, "ret": ret, "dif": dif,
        "gains": np.stack([a["attn_norm_w"][0], a["attn_norm_w"][1], a["ffn_norm_w"][0], a["ffn_norm_w"][1],
                           a["mem_norm_w"], a["norm_mix_g_2"][0], a["norm_xattn_g_2"][0], a["norm_mem_g_2"][0],
                           a["norm_mlp_g_2"][0], a["norm_final_g_2"]]),
        "rows": np.concatenate([a["ret_gn_w"].reshape(-1), a["diff_subln_w"].reshape(-1),
                                a["gdn_norm_g_2"].reshape(-1), a["gla_norm_g_2"].reshape(-1),
                                a["gdn_a_log_2"].reshape(-1), a["gdn_dt_bias_2"].reshape(-1),
                                a["diff_lambda_q1"].reshape(-1), a["diff_lambda_k1"].reshape(-1),
                                a["diff_lambda_q2"].reshape(-1), a["diff_lambda_k2"].reshape(-1)])[None, :],
        "vecs": np.concatenate([
            a["gdn_conv_w_2"][0].reshape(4, 24, 128).transpose(2, 1, 0).reshape(128, 96),
            a["gla_b_gate_2"][0].reshape(4, 128).T,
            np.concatenate([a["diff_q_norm_w"][0]] * 2)[:, None], np.concatenate([a["diff_k_norm_w"][0]] * 2)[:, None],
            np.concatenate([a["mem_q_norm_w"]] * 2, axis=1).T, np.concatenate([a["mem_k_norm_w"]] * 2, axis=1).T], axis=1),
    }
    return {k: np.ascontiguousarray(v) for k, v in arr.items()}


def kernel(**inputs):
    import concourse.bacc as _bacc
    from concourse.bass_utils import run_bass_kernel_spmd as _run

    nc = _bacc.Bacc("TRN2", target_bir_lowering=False, num_devices=1)
    arr = lay_out(inputs)
    W = {k: nc.dram_tensor(f"in_{k}", v.shape, mybir.dt.from_np(v.dtype), kind="ExternalInput").ap()
         for k, v in arr.items()}
    out = nc.dram_tensor("out_0", (1, T, D), F32, kind="ExternalOutput").ap()
    plan = build(nc, W, out, None)
    build(nc, W, out, plan)
    r = _run(nc, [{f"in_{k}": v for k, v in arr.items()}], core_ids=[0])
    return r.results[0]["out_0"]
```

```python
import math
from contextlib import ExitStack

import numpy as np

import concourse.bass as bass
from concourse import mybir

F32 = mybir.dt.float32
F32R = mybir.dt.float32r
ACT = mybir.ActivationFunctionType
ALU = mybir.AluOpType
AX = mybir.AxisListType

P = 128
T = 256
D = 1024
EPS = 1e-6
FFN = 2816
MIX = 768
UW = 1024
NR = 4
NH = 6
LA = 4
NSLOT = 20
LAMBDA_INIT = 0.8 - 0.6 * math.exp(-0.3)

GAINS = ["attn0", "attn1", "ffn0", "ffn1", "mem", "mix2", "xattn", "mem2", "mlp", "final"]
ROWS = {"ret_gn": (0, 768), "subln": (768, 128), "gdn_g": (896, 128), "gla_g": (1024, 256),
        "a_log": (1280, 8), "dt_bias": (1288, 8), "lq1": (1296, 64), "lk1": (1360, 64),
        "lq2": (1424, 64), "lk2": (1488, 64)}
NROW = 1552
VECS = {"conv": (0, 96), "b_gate": (96, 4), "dq": (100, 1), "dk": (101, 1), "mq": (102, 2), "mk": (104, 2)}
NVEC = 106
CONS = {"ident": (0, 128), "U": (128, 128), "S": (256, 128), "CO": (384, 256), "LM": (640, 768)}
NCON = 1408


def shape_constants():
    i = np.arange(128)
    same = (i[:, None] // 64) == (i[None, :] // 64)
    con = np.zeros((128, NCON), np.float32)
    con[:, 0:128] = np.eye(128)
    con[:, 128:256] = (i[:, None] <= i[None, :]) & same
    con[:, 256:384] = (i[:, None] > i[None, :]) & same
    for c in range(2):
        con[:, 384 + 128 * c:512 + 128 * c] = ((i // 64) == c)[:, None]
    for n in range(6):
        s = 1 << n
        blk = (i[:, None] // (2 * s) == i[None, :] // (2 * s)) & (i[:, None] // s % 2 == 0) & (i[None, :] // s % 2 == 1)
        con[:, 640 + 128 * n:768 + 128 * n] = blk
    pos = np.arange(256)
    dist = np.abs(pos[:, None] - pos[None, :]).astype(np.float64)
    seen = (pos[None, :] // 64) <= (pos[:, None] // 64)
    ret = np.zeros((128, 6, 384), np.float32)
    dif = np.zeros((128, 6, 384), np.float32)
    for h in range(6):
        lg = math.log(1.0 - 2.0 ** (-5.0 - h))
        dm = np.where(seen, np.exp(lg * dist), 0.0).T * 64 ** -0.5
        ret[:, h, 0:256] = dm[0:128, :]
        ret[:, h, 256:384] = dm[128:256, 128:256]
        slope = 2.0 ** (-8.0 * (h + 1) / 6)
        b = np.where(seen, -slope * dist, -1e30)
        dif[:, h, 0:128] = b[0:128, 0:128]
        dif[:, h, 128:384] = b[128:256, :]
    return con, ret.reshape(128, 2304), dif.reshape(128, 2304)


class Queue:

    def __init__(self, eng, sem, dry):
        self.eng, self.sem, self.n, self.seen, self.dry = eng, sem, 0, {}, dry

    def wait(self, toks):
        for t in toks:
            if t is None:
                continue
            if isinstance(t, list):
                self.wait(t)
            elif self.seen.get(id(t[0]), 0) < t[1]:
                self.seen[id(t[0])] = t[1]
                if not self.dry:
                    self.eng.wait_ge(t[0], t[1])

    def __call__(self, fn, *toks, sig=True):
        self.wait(toks)
        if sig:
            self.n += 1
        if not self.dry:
            ins = fn(self.eng)
            if sig:
                ins.then_inc(self.sem, 1)
        return (self.sem, self.n)

    def dma(self, fn, sem, value, *toks):
        self.wait(toks)
        if not self.dry:
            fn(self.eng).then_inc(sem, 16)
        return (sem, value)


def build(nc, W, out, scr, plan, stop=99):
    dry = plan is None
    order = []
    ctx = ExitStack()
    with ctx:
        sb = lambda n, s, d=F32: ctx.enter_context(nc.sbuf_tensor(n, s, d))
        sem = lambda n: ctx.enter_context(nc.semaphore(n))
        tag = "d" if dry else ""
        raw = sb(tag + "raw", [P, NR, UW])
        spl = sb(tag + "spl", [P, NH, 2, UW], F32R)
        X = sb(tag + "X", [P, 2, D])
        xs = sb(tag + "xs", [P, 2, 8, T], F32R)
        ys = sb(tag + "ys", [P, 2, 8, T], F32R)
        con = sb(tag + "con", [P, NCON])
        row = sb(tag + "row", [P, NROW])
        vec = sb(tag + "vec", [P, NVEC])
        sml = sb(tag + "sml", [P, 1536])
        gl2 = sb(tag + "gl2", [16, 512])
        sraw = sb(tag + "sraw", [P, 8, 32])
        sspl = sb(tag + "sspl", [P, 2, 8, 32], F32R)
        ar = sb(tag + "ar", [P, NSLOT, 1024])
        ps = [ctx.enter_context(nc.psum_tensor(f"{tag}ps{i}", [P, 512], F32)) for i in range(8)]

        PE = Queue(nc.tensor, sem(tag + "s_pe"), dry)
        AC = Queue(nc.scalar, sem(tag + "s_act"), dry)
        DV = Queue(nc.vector, sem(tag + "s_dve"), dry)
        PO = Queue(nc.gpsimd, sem(tag + "s_pool"), dry)
        SP = Queue(nc.sync, None, dry)
        s_raw = [sem(f"{tag}s_raw{i}") for i in range(NR)]
        s_ld = [sem(f"{tag}s_ld{i}") for i in range(48)]
        s_out = sem(tag + "s_out")
        ld = [0]

        def load(dst, src, *toks, q=None):
            s = s_ld[ld[0]]
            ld[0] += 1
            return (q or PO).dma(lambda e: e.dma_start(dst, src), s, 16, *toks)

        sm = [0]

        def small(n):
            a = sm[0]
            sm[0] += n
            assert sm[0] <= 1536
            return sml[:, a:a + n]

        slots = [(0, []) for i in range(40)] if dry else [(i, []) for i in range(NSLOT)]

        class Slot:

            def __init__(self):
                self.i, self.free = slots.pop(0)
                self.v = ar[:, self.i, :]
                self.v2 = ar[:, self.i, :].rearrange("p (t n) -> p t n", t=2)

            def give(self, *toks):
                slots.append((self.i, list(toks)))

        banks = [(i, []) for i in range(8)]

        class Bank:

            def __init__(self):
                self.i, self.free = banks.pop(0)
                self.v = ps[self.i][:, :]

            def g(self, n):
                return ps[self.i][:, :].rearrange("p (a b) -> p a b", a=n)

            def give(self, *toks):
                banks.append((self.i, list(toks)))

        raw_tok, lo_tok, pe_tok, cnt = {}, {}, {}, [0] * NR
        nsplit, hi_tok = [0, 0], {}

        def fetch(u, *toks):
            s = u % NR
            src = plan[u]
            if len(src.shape) == 4:
                dst = raw[:, s, :].rearrange("p (a b c) -> p a b c", a=src.shape[1], b=2)
                parts = [(dst[:, :, i, :], src[:, :, i, :]) for i in range(2)]
            else:
                parts = [(raw[:, s, :].rearrange("p (a b) -> p a b", a=2), src)]
            for dst, src in parts:
                cnt[s] += 16
                raw_tok[u] = SP.dma(lambda e: e.dma_start(dst, src), s_raw[s], cnt[s], *toks)

        def get_gain(name, q=None):
            s = Slot()
            return s, load(s.v, W["gains"][GAINS.index(name):GAINS.index(name) + 1, :].partition_broadcast(P),
                           s.free, q=q)

        xin = lambda a: a.rearrange("b (t p) d -> p (b t) d", p=P)
        mem_s = [Slot(), Slot()]
        m_tok = [load(mem_s[0].v, W["mem"][0, 0:P, :], q=SP)]
        t_con = load(con[:, 0:128], W["con"][:, 0:128], q=AC)
        g_mem = get_gain("mem", AC)
        nf = min(NR, len(plan)) if not dry else 0
        for u in range(min(1, nf)):
            fetch(u)
        m_tok.append(load(mem_s[1].v, W["mem"][0, P:2 * P, :], q=SP))
        for u in range(1, nf):
            fetch(u)
        x_tok = load(X[:, :, :], xin(W["x"]), q=SP)
        t_vec = load(vec[:, :], W["vecs"])
        ident = con[:, 0:128]
        cU = con[:, 128:256]
        cS = con[:, 256:384]
        R = lambda n: row[:, ROWS[n][0]:ROWS[n][0] + ROWS[n][1]]
        V = lambda n, k=0, w=1: vec[:, VECS[n][0] + k:VECS[n][0] + k + w]
        neg = small(32)
        t_neg = PO(lambda e: e.memset(neg, -0.5))

        def bc(ap, n):
            return ap.unsqueeze(ap.ndim).to_broadcast(list(ap.shape) + [n])

        def bm(ap, n):
            return ap.unsqueeze(1).to_broadcast([ap.shape[0], n] + list(ap.shape[1:]))

        def split_hi(u):
            s, h = u % NR, u % NH
            hi_tok[u] = AC(lambda e: e.copy(spl[:, h, 0, :], raw[:, s, :]), raw_tok[u], pe_tok.get(u - NH))

        def split_lo(u):
            s, h = u % NR, u % NH
            lo_tok[u] = DV(lambda e: e.tensor_tensor(spl[:, h, 1, :], raw[:, s, :],
                                                     spl[:, h, 0, :].bitcast(F32), ALU.subtract), hi_tok[u])
            if u + NR < len(plan):
                fetch(u + NR, lo_tok[u])

        def splits(hi, lo):
            if not dry:
                for u in range(nsplit[1], max(hi, lo)):
                    if nsplit[0] < min(hi, len(plan)):
                        split_hi(nsplit[0])
                        nsplit[0] += 1
                    if nsplit[1] < min(lo, len(plan)):
                        split_lo(nsplit[1])
                        nsplit[1] += 1

        def unit(src):
            u = len(order)
            order.append(src)
            splits(u + 1, u + 1)
            v = spl[:, u % NH, :, :].rearrange("p l (a b) -> p l a b", a=2)
            return u, v[:, 0], v[:, 1]

        def product(u, xin_, kt, t, w_hi, w_lo, bank, start, stop, last):
            xh, xl = xin_[:, 0, kt, t * P:(t + 1) * P], xin_[:, 1, kt, t * P:(t + 1) * P]
            PE(lambda e: e.matmul(bank, xh, w_hi, start=start, stop=False), lo_tok.get(u), sig=False)
            PE(lambda e: e.matmul(bank, xh, w_lo, start=False, stop=False), sig=False)
            return PE(lambda e: e.matmul(bank, xl, w_hi, start=False, stop=stop), sig=last)

        def ahead():
            splits(len(order) + LA + 1, len(order) + LA)

        class Pre:

            def __init__(self, piece, after=None):
                self.piece, self.tok, self.after = piece, {}, after or (lambda: None)

            def need(self, t, k):
                if (t, k) not in self.tok:
                    self.piece(t, k)

            def all(self):
                for t in range(2):
                    for k in range(2):
                        self.need(t, k)

        def of_tile(xtok, t, kt):
            if isinstance(xtok, Pre):
                xtok = xtok.tok
            return xtok[(t, kt // 4)] if isinstance(xtok, dict) else xtok

        def cols(src_of, xin_, xtok, done, groups=(1, 1, 1, 1), pre=None):
            b = [Bank(), Bank()]
            k0 = 0
            for g in groups:
                if pre and k0 == 0:
                    pre.need(0, 0)
                    pre.need(0, 1)
                us = [unit(src_of(k0 + i)) for i in range(g)]
                toks = []
                for t in range(2):
                    if pre and k0 == 0 and t == 1:
                        pre.all()
                    if k0 == 0:
                        PE.wait([b[t].free])
                    for i, (u, hi, lo) in enumerate(us):
                        for j in range(2):
                            kt = 2 * (k0 + i) + j
                            if pre and k0 == 0 and t == 0 and kt in (3, 4):
                                pre.need(1, kt - 3)
                            PE.wait([of_tile(xtok, t, kt)])
                            tok = product(u, xin_, kt, t, hi[:, j], lo[:, j], b[t].v, kt == 0, kt == 7, j == 1)
                        if t == 1:
                            pe_tok[u] = tok
                    toks.append(tok)
                if pre and k0 == 0:
                    pre.after()
                k0 += g
                if k0 == 4:
                    done(b, toks)
                ahead()
                yield

        def rows_(w, kts, xin_, off, xtok, acc, first, last, groups=None, pre=None):
            kts = list(kts)
            n0 = 0
            for g in groups or (1,) * len(kts):
                if pre and n0 == 0:
                    pre.need(0, 0)
                    pre.need(0, 1)
                us = [unit(w[kt * P:(kt + 1) * P, :].rearrange("p (a b) -> p a b", a=2)) for kt in kts[n0:n0 + g]]
                toks = []
                for t in range(2):
                    if pre and n0 == 0 and t == 1:
                        pre.all()
                    for i, (u, hi, lo) in enumerate(us):
                        n = n0 + i
                        if pre and n0 == 0 and t == 0 and n in (1, 2):
                            pre.need(1, n - 1)
                        PE.wait([of_tile(xtok, t, off + n)])
                        for j in range(2):
                            if n == 0:
                                PE.wait([acc[t][j].free])
                            tok = product(u, xin_, off + n, t, hi[:, j], lo[:, j], acc[t][j].v,
                                          first and n == 0, last and n == len(kts) - 1, j == 1)
                        if t == 1:
                            pe_tok[u] = tok
                    toks.append(tok)
                if pre and n0 == 0:
                    pre.after()
                n0 += g
                ahead()
                yield toks

        def block(w, c0):
            return lambda k: w[k * 256:(k + 1) * 256, c0:c0 + 512].rearrange("(a p) n -> p a n", p=P)

        def run(g):
            for _ in g:
                pass

        def chain(*gs):
            for g in gs:
                yield from g

        def weave(main, bg, n=1, counts=None):
            for i, _ in enumerate(main):
                for _ in range(counts[i] if counts else n):
                    next(bg, None)
            if not counts:
                run(bg)

        def take(g, n):
            for _ in range(n):
                next(g, None)
                yield

        def both(*gs):
            gs = list(gs)
            while gs:
                for g in list(gs):
                    if next(g, g) is g:
                        gs.remove(g)
                    else:
                        yield

        xuse = {id(xs): [], id(ys): []}

        def halves(src, dst, k0, nk, t, *toks):
            b = Bank()
            PE.wait([b.free])
            for j in range(nk):
                tok = PE(lambda e, j=j: e.transpose(b.v[:, j * P:(j + 1) * P], src[:, j * P:(j + 1) * P], ident),
                         *toks, t_con, sig=(j == nk - 1))
            bv = b.g(4)[:, 0:nk, :]
            o = lambda l: dst[:, l, k0:k0 + nk, t * P:(t + 1) * P]
            a = AC(lambda e: e.copy(o(0), bv), tok, *xuse[id(dst)])
            d = DV(lambda e: e.tensor_tensor(o(1), bv, o(0).bitcast(F32), ALU.subtract), a)
            b.give(d)
            return d

        def spread(src, dst, toks, after=None):
            def piece(t, k):
                p.tok[(t, k)] = halves(src(t, k), dst, 4 * k, 4, t, toks(t, k))
            p = Pre(piece, after)
            return p

        def rsqrt(ss, n, scale, eps, tok):
            m, r = small(n), small(n)
            a = DV(lambda e: e.tensor_scalar(m, ss, scale, eps, ALU.mult, ALU.add), tok)
            return r, PO(lambda e: e.tensor_tensor(r, m, neg[:, 0:n], ALU.pow), a, t_neg)

        def norm(src, g, dst, stoks, acc=None, xt=None):
            gi, gt = g
            hb, rs = [Slot(), Slot()], []
            rest = [None, None]
            c = [slice(k * 512, (k + 1) * 512) for k in range(2)]
            ready = {}

            def prep(t):
                st = []
                for k in range(2):
                    if acc is None:
                        st.append(stoks[t])
                    else:
                        v = X[:, t, c[k]]
                        d = DV(lambda e: e.tensor_tensor(v, acc[0][t][k].v, v, ALU.add), acc[1][t], xt[t])
                        acc[0][t][k].give(d)
                        st.append(d)
                    ready[(t, k)] = DV(lambda e: e.tensor_tensor(hb[t].v[:, c[k]], src(t)[:, c[k]], gi.v[:, c[k]],
                                                                 ALU.mult), st[k], gt, hb[t].free)
                if acc is not None:
                    xt[t] = st
                rest[t] = st
                if t == 1:
                    gi.give(ready[(t, 1)])

            def piece(t, k):
                if (t, 0) not in ready:
                    prep(t)
                p.tok[(t, k)] = halves(hb[t].v[:, c[k]], dst, 4 * k, 4, t, ready[(t, k)])

            def after():
                for t in range(2):
                    ss = small(1)
                    a = AC(lambda e: e.activation(hb[t].v, src(t), ACT.Square, accum_out=ss), p.tok[(t, 0)],
                           p.tok[(t, 1)], rest[t])
                    rs.append(rsqrt(ss, 1, 1.0 / D, EPS, a))
                    hb[t].give(a)
            p = Pre(piece, after)
            p.prep = prep
            return p, rs

        def evac(dst_of, rs):
            out_ = {}

            def done(b, toks):
                for t in range(2):
                    dst, w = dst_of(t)
                    if rs is None:
                        a = AC(lambda e: e.copy(dst, b[t].v), toks[t], w)
                    else:
                        a = AC(lambda e: e.mul(dst, b[t].v, rs[t][0]), toks[t], w, rs[t][1])
                    b[t].give(a)
                    out_[t] = a
            return done, out_

        def to_slot(src_of, xin_, xtok, box, rs=None, groups=(1, 1, 1, 1), pre=None):
            def g():
                s = Slot()
                done, o = evac(lambda t: (s.v2[:, t, :], s.free), rs)

                def finish(b, toks):
                    done(b, toks)
                    if isinstance(box, tuple):
                        box[0][box[1]] = (s, [o[0], o[1]])
                    else:
                        box.append((s, [o[0], o[1]]))
                yield from cols(src_of, xin_, xtok, finish, groups, pre)
            return g()

        def residual(w, nk, xin_, pre, groups=(3, 1, 1, 3)):
            acc = [[Bank(), Bank()], [Bank(), Bank()]]
            for toks in rows_(w, range(nk), xin_, 0, pre, acc, True, True, groups, pre):
                pass
            return acc, toks

        FIRST = (3, 1)

        def group_rs(v, n, w, scale, eps, tok, mul=None):
            s = Slot()
            sq = s.v[:, 0:n * w]
            p = AC(lambda e: e.activation(sq, v, ACT.Square), tok, s.free)
            ss = small(n)
            d = DV(lambda e: e.tensor_reduce(ss, sq.rearrange("p (a b) -> p a b", b=w), AX.X, ALU.add), p)
            s.give(d)
            r, rt = rsqrt(ss, n, scale, eps, d)
            if mul is not None:
                r2 = small(n)
                rt = DV(lambda e: e.tensor_scalar(r2, r, mul, None, ALU.mult), rt)
                r = r2
            return r, rt

        def softmax_mem(t, sc, toks_b, norm_):
            s = Slot()
            m, nm, sm_, r = small(4), small(4), small(4), small(4)
            out_ = []
            v = s.v.rearrange("p (h n) -> p h n", h=4)
            for i, b in enumerate(sc):
                d = DV(lambda e: e.tensor_reduce(m[:, 2 * i:2 * i + 2], b.g(2), AX.X, ALU.max), toks_b[i])
                d = DV(lambda e: e.tensor_scalar(nm[:, 2 * i:2 * i + 2], m[:, 2 * i:2 * i + 2], -1.0, None,
                                                 ALU.mult), d)
                for k in range(2):
                    h = 2 * i + k
                    a = AC(lambda e: e.activation(s.v[:, h * 256:(h + 1) * 256], b.g(2)[:, k, :], ACT.Exp,
                                                  bias=nm[:, h:h + 1], accum_out=sm_[:, h:h + 1]), d, s.free)
                b.give(a)
                hs = slice(2 * i, 2 * i + 2)
                d = DV(lambda e: e.reciprocal(r[:, hs], sm_[:, hs]), a)
                if norm_:
                    d = DV(lambda e: e.tensor_tensor(v[:, hs, :], v[:, hs, :], bc(r[:, hs], 256), ALU.mult), d)
                out_.append(d if norm_ else a)
            return s, out_, r, d

        def transposed8(src, tok, dst, dfree, eng2=True):
            r = []
            for k in range(2):
                b = Bank()
                PE.wait([b.free, tok[k], t_con])
                for j in range(4):
                    p = PE(lambda e: e.transpose(b.v[:, j * P:(j + 1) * P],
                                                 src[:, (4 * k + j) * P:(4 * k + j + 1) * P], ident), sig=(j == 3))
                a = AC(lambda e: e.copy(dst[:, k * 512:(k + 1) * 512], b.v), p, dfree)
                b.give(a)
                r.append(a)
            return r

        def mem_attention(qc, qtok, kT, v, ktok, O, Otok, wq):
            wcol = small(1)
            wt = DV(lambda e: e.tensor_scalar(wcol, wq, 0.125, None, ALU.mult), t_vec)
            s = Slot()
            b = Bank()
            ht = []
            for t in range(2):
                r, rt = group_rs(qc(t), 4, 64, 1.0 / 64, EPS, qtok[t])
                hv = s.v[:, t * 256:(t + 1) * 256].rearrange("p (a b) -> p a b", b=64)
                ht.append(DV(lambda e: e.tensor_tensor(hv, qc(t).rearrange("p (a b) -> p a b", b=64), bc(r, 64),
                                                       ALU.mult), rt, s.free))
            yield
            yield
            for t in range(2):
                for f in range(2):
                    PE.wait([b.free, ht[t], t_con])
                    p = PE(lambda e: e.transpose(b.v[:, f * 256 + t * P:f * 256 + (t + 1) * P],
                                                 s.v[:, t * 256 + f * P:t * 256 + (f + 1) * P], ident),
                           sig=(t == 1 and f == 1))
            qT = s.v[:, 512:1024]
            a = AC(lambda e: e.mul(qT, b.v, wcol), p, wt)
            b.give(a)
            yield
            W_ = []
            for t in range(2):
                sc, st = [], []
                for k in range(2):
                    b = Bank()
                    sc.append(b)
                    p0 = 64 * k
                    for f in range(2):
                        PE.wait([b.free, a, ktok])
                        p = PE(lambda e: e.matmul(b.g(2)[:, f, :], qT[p0:p0 + 64, f * 256 + t * P:f * 256 + (t + 1) * P],
                                                  kT[p0:p0 + 64, f, :], start=True, stop=True), sig=(f == 1))
                    st.append(p)
                W_.append(softmax_mem(t, sc, st, False))
                yield
            s.give((PE.sem, PE.n))
            WT = []
            for t in range(2):
                w, wtok, rc, rct = W_[t]
                wT = Slot()
                tt = transposed8(w.v, wtok, wT.v, wT.free)
                w.give((PE.sem, PE.n))
                yield
                WT.append((wT, tt, rc, rct))
            for t in range(2):
                wT, tt, rc, rct = WT[t]
                ob = Bank()
                nh = lambda h: 2 * (h % 2) + h // 2
                for h in range(4):
                    for m in range(2):
                        PE.wait([ob.free, tt])
                        p = PE(lambda e: e.matmul(ob.v[:, h * 64:(h + 1) * 64],
                                                  wT.v[:, (2 * nh(h) + m) * P:(2 * nh(h) + m + 1) * P],
                                                  v(m)[:, h * 64:(h + 1) * 64], start=(m == 0), stop=(m == 1)),
                               sig=(h == 3 and m == 1))
                wT.give(p)
                ov = lambda a_: a_.rearrange("p (f k n) -> p f k n", f=2, k=2)
                rv = rc.rearrange("p (k f) -> p f k", k=2)
                for f in range(2):
                    o = DV(lambda e: e.tensor_tensor(ov(O[t].v[:, 768:1024])[:, f], ov(ob.v[:, 0:256])[:, f],
                                                     bc(rv[:, f, :], 64), ALU.mult), p, O[t].free, rct)
                ob.give(o)
                Otok[t].append(o)

        def mem_keys(box, kv, wk):
            s, tk = kv
            ht = []
            for t in range(2):
                kk = s.v2[:, t, 0:256]
                r, rt = group_rs(kk, 4, 64, 1.0 / 64, EPS, tk[t])
                v3 = kk.rearrange("p (a b) -> p a b", b=64)
                ht.append(DV(lambda e: e.tensor_tensor(v3, v3, bc(r, 64), ALU.mult), rt))
            yield
            yield
            b = Bank()
            for t in range(2):
                for f in range(2):
                    PE.wait([b.free, ht[t], t_con])
                    p = PE(lambda e: e.transpose(b.v[:, f * 256 + t * P:f * 256 + (t + 1) * P],
                                                 s.v2[:, t, f * P:(f + 1) * P], ident), sig=(t == 1 and f == 1))
            a = AC(lambda e: e.mul(s.v2[:, :, 0:256], b.g(2), wk), p, t_vec)
            b.give(a)
            box.append(a)
            yield

        def out_norm(O, Otok, n, w, mul, fac):
            for t in range(2):
                ov = O[t].v[:, 0:n * w]
                o3 = ov.rearrange("p (a b) -> p a b", b=w)
                r, rt = group_rs(ov, n, w, 1.0 / w, EPS, Otok[t], mul)
                d = DV(lambda e: e.tensor_tensor(o3, o3, bc(r, w), ALU.mult), rt)
                f, ft = fac(t)
                Otok[t].append(DV(lambda e: e.tensor_tensor(o3, o3, f, ALU.mult), d, ft))
                yield

        xt = [x_tok, x_tok]

        mtok, mrs = norm(lambda t: mem_s[t].v, g_mem, ys, m_tok)
        mtok.need(0, 0)
        g_x = get_gain("attn0")

        kvs, mks = [], []
        run(to_slot(block(W["w_mem_kv"][0], 0), ys, mtok, kvs, mrs, FIRST, mtok))
        for t in range(2):
            mem_s[t].give((DV.sem, DV.n), (AC.sem, AC.n))
        t_row = load(row[:, :], W["rows"].partition_broadcast(P), (PE.sem, PE.n))
        t_con2 = load(con[:, 128:NCON], W["con"][:, 128:NCON])
        xtok, xrs = norm(lambda t: X[:, t, :], g_x, xs, xt)

        def out_banks(o_of, O, Otok, hp):
            b = Bank()
            for k in range(2):
                o_of(b, 2 * hp + k, k)
            tok = (PE.sem, PE.n)
            bv = b.v.rearrange("p (k t n) -> p k t n", k=2, t=2)
            for t in range(2):
                o = O[t].v[:, hp * 256:(hp + 1) * 256].rearrange("p (k n) -> p k n", k=2)
                a = AC(lambda e: e.copy(o, bv[:, :, t, :]), tok, O[t].free)
                Otok[t].append(a)
            b.give(a)

        def retention(B, O, Otok):
            dm = [Slot() for _ in range(3)]
            dt_ = [load(dm[i].v[:, 0:768], W["ret"][:, i * 768:(i + 1) * 768], dm[i].free) for i in range(3)]
            qk = [Slot(), Slot()]
            qt = [[], []]
            src = [[(0, 0), (0, 128), (0, 256)], [(0, 384), (1, 0), (1, 128)]]
            for w in range(2):
                for f0, nf in ((0, 2), (2, 1)):
                    b = Bank()
                    PE.wait([b.free, t_con])
                    for f in range(f0, f0 + nf):
                        si, c = src[w][f]
                        for t in range(2):
                            p = PE(lambda e: e.transpose(b.v[:, (f - f0) * 256 + t * P:(f - f0) * 256 + (t + 1) * P],
                                                         B[si][0].v2[:, t, c:c + P], ident), B[si][1][t])
                    dst = qk[w].v[:, f0 * 256:(f0 + nf) * 256]
                    if w == 0:
                        a = AC(lambda e: e.copy(dst, b.v[:, 0:nf * 256]), p, qk[w].free)
                    else:
                        a = DV(lambda e: e.tensor_copy(dst, b.v[:, 0:nf * 256]), p, qk[w].free)
                    b.give(a)
                    qt[w].append(a)
            yield
            vof = lambda h, t: (B[1][0].v2[:, t, 256 + h * 128:384 + h * 128] if h < 2
                                else B[2][0].v2[:, t, (h - 2) * 128:(h - 1) * 128])
            spt = [None] * 6
            for h in range(6):
                f, p0 = h // 2, 64 * (h % 2)
                b = Bank()
                PE.wait([b.free, qt])
                q, k = qk[0].v[p0:p0 + 64, f * 256:(f + 1) * 256], qk[1].v[p0:p0 + 64, f * 256:(f + 1) * 256]
                PE(lambda e: e.matmul(b.v[:, 0:256], k[:, 0:128], q, start=True, stop=True), sig=False)
                p = PE(lambda e: e.matmul(b.v[:, 256:384], k[:, 128:256], q[:, 128:256], start=True, stop=True))
                dv = dm[h // 2].v[:, (h % 2) * 384:(h % 2) * 384 + 384]
                d = DV(lambda e: e.tensor_tensor(dv, b.v[:, 0:384], dv, ALU.mult), p, dt_)
                b.give(d)
                spt[h] = d
                if h % 2:
                    yield
            for w in range(2):
                qk[w].give((PE.sem, PE.n))

            def o_of(b, h, k):
                s = dm[h // 2].v[:, (h % 2) * 384:(h % 2) * 384 + 384]
                PE.wait([b.free, spt[h], B[1][1], B[2][1]])
                bo = lambda t: b.v[:, (2 * k + t) * P:(2 * k + t + 1) * P]
                PE(lambda e: e.matmul(bo(0), s[:, 0:128], vof(h, 0), start=True, stop=True))
                PE(lambda e: e.matmul(bo(1), s[:, 128:256], vof(h, 0), start=True, stop=False))
                PE(lambda e: e.matmul(bo(1), s[:, 256:384], vof(h, 1), start=False, stop=True))
            for hp in range(3):
                out_banks(o_of, O, Otok, hp)
                dm[hp].give((PE.sem, PE.n))
                yield

        def ret_gates(B):
            for t in range(2):
                s = Slot()
                for a0, n, sl, c in ((0, 512, 3, 0), (512, 256, 4, 0)):
                    g = B[sl][0].v2[:, t, c:c + n]
                    th = s.v[:, a0:a0 + n]
                    a = AC(lambda e: e.activation(th, g, ACT.Tanh, scale=0.5), B[sl][1][t], s.free)
                    d = DV(lambda e: e.scalar_tensor_tensor(th, th, 1.0, g, ALU.add, ALU.mult), a)
                    d = DV(lambda e: e.scalar_tensor_tensor(th, th, 0.5, R("ret_gn")[:, a0:a0 + n], ALU.mult, ALU.mult),
                           d, t_row)
                gates.append((s, d))
            yield

        B = {}
        g1 = get_gain("ffn0")

        def u_block(l, i, pre=None):
            return to_slot(block(W["w_in"][l], 512 * i), xs, xtok, (B, i), xrs, FIRST if pre else (1,) * 4, pre)
        weave(chain(u_block(0, 0, xtok), u_block(0, 1)), mem_keys(mks, kvs[0], V("mk", 0)))
        O = [Slot(), Slot()]
        Otok, Otok2 = [[], []], [[], []]
        ret = retention(B, O, Otok)
        gates = []
        weave(u_block(0, 4), ret, counts=(1, 1, 1, 1))
        qc = lambda t: B[4][0].v2[:, t, 256:512]
        vv = lambda i: (lambda m: kvs[i][0].v2[:, m, 256:512])
        kT3 = lambda i: kvs[i][0].v2[:, :, 0:256]
        ma = mem_attention(qc, B[4][1], kT3(0), vv(0), [mks[0], kvs[0][1]], O, Otok2, V("mq", 0))
        weave(chain(u_block(0, 2), u_block(0, 3), to_slot(block(W["w_mem_kv"][1], 0), ys, mtok, kvs, mrs)),
              chain(take(ma, 5), ret, ret_gates(B),
                    out_norm(O, Otok, 6, 128, None, lambda t: (gates[t][0].v[:, 0:768].rearrange(
                        "p (a b) -> p a b", b=128), gates[t][1])), ma))
        for g_, _ in gates:
            g_.give((DV.sem, DV.n))
        xuse[id(xs)] = [(PE.sem, PE.n)]
        xuse[id(ys)] = [(PE.sem, PE.n)]
        fin = [(PE.sem, PE.n), (DV.sem, DV.n), (AC.sem, AC.n), (PO.sem, PO.n)]
        for b_ in B.values():
            b_[0].give(*fin)
        kvs[0][0].give(*fin)
        acc = residual(W["w_out"][0], 8, xs, spread(lambda t, k: O[t].v[:, k * 512:(k + 1) * 512], xs,
                                                    lambda t, k: Otok[t] + Otok2[t]))
        for t in range(2):
            O[t].give((PE.sem, PE.n))
        xuse[id(xs)] = [(PE.sem, PE.n)]

        def ffn(l, g, acc0):
            xtok, xrs = norm(lambda t: X[:, t, :], g, xs, None, acc0, xt)
            hr, h2 = [], []

            def factors():
                for t in range(2):
                    a_, b_ = small(1), small(1)
                    r, rt = xrs[t]
                    d1 = DV(lambda e: e.tensor_scalar(a_, r, 0.5, None, ALU.mult), rt)
                    d2 = DV(lambda e: e.tensor_tensor(b_, a_, r, ALU.mult), d1)
                    hr.append((a_, d1))
                    h2.append((b_, d2))
            acc = []
            wg = W["w_gate_up"][l].rearrange("(k p) (g n) -> p k g n", p=P, g=2)
            nb = FFN // 256
            act = {}

            def gate_up(b, groups):
                s = Slot()
                box = act[b] = (s, [])

                def done(bk, toks):
                    if not b:
                        factors()
                    for t in range(2):
                        w = bk[t].v
                        th = s.v2[:, t, 256:512]
                        o = s.v2[:, t, 0:256]
                        a = AC(lambda e: e.activation(th, w[:, 0:256], ACT.Tanh, scale=hr[t][0]), toks[t], s.free, hr[t][1])
                        d = DV(lambda e: e.scalar_tensor_tensor(th, th, 1.0, w[:, 0:256], ALU.add, ALU.mult), a)
                        d = DV(lambda e: e.scalar_tensor_tensor(o, th, h2[t][0], w[:, 256:512], ALU.mult, ALU.mult), d, h2[t][1])
                        bk[t].give(d)
                        box[1].append(d)
                return cols(lambda k: wg[:, 2 * k:2 * k + 2, :, b * 256:(b + 1) * 256], xs, xtok, done, groups,
                            None if b else xtok)

            def turn(b):
                s, tk = act[b]
                bk = Bank()
                PE.wait([bk.free])
                for t in range(2):
                    for f in range(2):
                        p = PE(lambda e: e.transpose(bk.v[:, f * 256 + t * P:f * 256 + (t + 1) * P],
                                                     s.v2[:, t, f * P:(f + 1) * P], ident), tk[t])
                s.give(p)
                k0 = 2 * (b % 4)
                o = lambda l_: ys[:, l_, k0:k0 + 2, :]
                a = AC(lambda e: e.copy(o(0), bk.g(2)), p, yfree[b % 4])
                d = DV(lambda e: e.tensor_tensor(o(1), bk.g(2), o(0).bitcast(F32), ALU.subtract), a)
                bk.give(d)
                return d
            yfree = [list(xuse[id(ys)]) for _ in range(4)]
            yt = {}

            def down(b):
                last = b == nb - 1
                for n, toks in enumerate(rows_(W["w_down"][l], [2 * b, 2 * b + 1], ys, 2 * (b % 4), yt[b], acc,
                                               b == 0, last, (2,) if last else None)):
                    if n == 0 and not last:
                        yt[b + 1] = turn(b + 1)
                yfree[b % 4] = [toks[1]]
                return toks
            for b in range(nb):
                if b == 1:
                    acc.extend([[Bank(), Bank()], [Bank(), Bank()]])
                for k, _ in enumerate(gate_up(b, (1, 1, 1, 1) if b else FIRST)):
                    if b == 1 and k == 1:
                        yt[0] = turn(0)
                if b:
                    down(b - 1)
            xuse[id(xs)] = [pe_tok[len(order) - 3]] if not dry else []
            toks = down(nb - 1)
            xuse[id(ys)] = [toks[1]]
            return acc, toks


        def done_early():
            b, bt = acc
            for t in range(2):
                for k in range(2):
                    v = X[:, t, k * 512:(k + 1) * 512]
                    xt[t] = DV(lambda e: e.tensor_tensor(v, b[t][k].v, v, ALU.add), bt[t], xt[t])
            return SP.dma(lambda e: e.dma_start(xin(out), X[:, :, :]), s_out, 16, xt)

        if stop >= 2:
            g2 = get_gain("attn1")
            gm2 = get_gain("mem2")
            mem_s = [Slot(), Slot()]
            m_tok = [load(mem_s[t].v, W["mem2"][0, t * P:(t + 1) * P, :], mem_s[t].free) for t in range(2)]
            acc = ffn(0, g1, acc)
            kv_out = []

        def diff(B, O, Otok):
            bi = [Slot() for _ in range(3)]
            bt = [load(bi[i].v[:, 0:768], W["dif"][:, i * 768:(i + 1) * 768], bi[i].free) for i in range(3)]
            lam = small(4)
            jk = small(64)
            d = DV(lambda e: e.tensor_tensor(jk, R("lq1"), R("lk1"), ALU.mult), t_row)
            d = DV(lambda e: e.tensor_reduce(lam[:, 0:1], jk, AX.X, ALU.add), d)
            jk2 = small(64)
            d = DV(lambda e: e.tensor_tensor(jk2, R("lq2"), R("lk2"), ALU.mult), d)
            d = DV(lambda e: e.tensor_reduce(lam[:, 1:2], jk2, AX.X, ALU.add), d)
            a = AC(lambda e: e.activation(lam[:, 2:4], lam[:, 0:2], ACT.Exp), d)
            nlam = small(1)
            d = DV(lambda e: e.tensor_tensor(nlam, lam[:, 3:4], lam[:, 2:3], ALU.subtract), a)
            nl = small(1)
            tl = DV(lambda e: e.tensor_scalar(nl, nlam, -LAMBDA_INIT, None, ALU.add), d)
            wq = small(1)
            tq = DV(lambda e: e.tensor_scalar(wq, V("dq"), 0.125, None, ALU.mult), t_vec)
            qk = [Slot() for _ in range(3)]
            qt = []

            def prep(i):
                s, tk = B[i]
                v3 = s.v.rearrange("p (a b) -> p a b", b=64)
                r, rt = group_rs(s.v, 16, 64, 1.0 / 64, EPS, tk)
                d = DV(lambda e: e.tensor_tensor(v3, v3, bc(r, 64), ALU.mult), rt)
                yield
                for f0 in (0, 2):
                    b = Bank()
                    PE.wait([b.free, d, t_con])
                    for f in range(2):
                        for t in range(2):
                            p = PE(lambda e: e.transpose(b.v[:, f * 256 + t * P:f * 256 + (t + 1) * P],
                                                         s.v2[:, t, (f0 + f) * P:(f0 + f + 1) * P], ident))
                    is_q = 4 * i + f0 < 6
                    a = AC(lambda e: e.mul(qk[i].v[:, f0 * 256:(f0 + 2) * 256], b.v, wq if is_q else V("dk")),
                           p, tq, qk[i].free)
                    b.give(a)
                    qt.append(a)
                s.give(p)
            ft = lambda n: qk[n // 4].v[:, (n % 4) * 256:(n % 4 + 1) * 256]
            vof = lambda h, t: (B[3][0].v2[:, t, h * P:(h + 1) * P] if h < 4
                                else B[4][0].v2[:, t, (h - 4) * P:(h - 3) * P])
            st = {}

            def scores(h):
                s = Slot()
                tk = []
                mx, nm, su = small(4), small(4), small(4)
                sv = s.v[:, 0:768].rearrange("p (c n) -> p c n", c=2)
                part = lambda it: sv[:, :, 0:128] if it == 0 else sv[:, :, 128:384]
                bias = bi[h // 2].v[:, (h % 2) * 384:(h % 2) * 384 + 384]
                for c in range(2):
                    b = Bank()
                    PE.wait([b.free, qt[h // 2], qt[(6 + h) // 2]])
                    q, k = ft(h)[64 * c:64 * c + 64, :], ft(6 + h)[64 * c:64 * c + 64, :]
                    PE(lambda e: e.matmul(b.v[:, 0:128], q[:, 0:128], k[:, 0:128], start=True, stop=True), sig=False)
                    p = PE(lambda e: e.matmul(b.v[:, 128:384], q[:, 128:256], k, start=True, stop=True))
                    d = DV(lambda e: e.tensor_tensor(sv[:, c, :], b.v[:, 0:384], bias, ALU.add), p, bt, s.free)
                    b.give(d)
                    tk.append(d)
                for it in range(2):
                    d = DV(lambda e: e.tensor_reduce(mx[:, 2 * it:2 * it + 2], part(it), AX.X, ALU.max), tk)
                d = DV(lambda e: e.tensor_scalar(nm, mx, -1.0, None, ALU.mult), d)
                for it in range(2):
                    for c in range(2):
                        a = AC(lambda e: e.activation(part(it)[:, c, :], part(it)[:, c, :], ACT.Exp,
                                                      bias=nm[:, 2 * it + c:2 * it + c + 1],
                                                      accum_out=su[:, 2 * it + c:2 * it + c + 1]), d)
                st[h] = (s, a, su, part)

            def combine(h):
                s, a, su, part = st[h]
                rc, rc2 = small(4), small(4)
                d = DV(lambda e: e.reciprocal(rc, su), a)
                d = DV(lambda e: e.tensor_scalar(rc2, rc, nl, None, ALU.mult), d, tl)
                for it in range(2):
                    pv = part(it)
                    d2 = AC(lambda e: e.mul(pv[:, 0, :], pv[:, 0, :], rc[:, 2 * it:2 * it + 1]), d)
                    d2 = DV(lambda e: e.scalar_tensor_tensor(pv[:, 0, :], pv[:, 1, :], rc2[:, 2 * it + 1:2 * it + 2],
                                                             pv[:, 0, :], ALU.mult, ALU.add), d2)
                st[h] = (s, d2)

            def turn(h):
                s, d = st[h]
                b = Bank()
                PE.wait([b.free, d, t_con])
                for j, c in enumerate((0, 128, 256)):
                    p = PE(lambda e: e.transpose(b.v[:, j * P:(j + 1) * P], s.v[:, c:c + P], ident), sig=(j == 2))
                a = AC(lambda e: e.copy(s.v[:, 384:768], b.v[:, 0:384]), p)
                b.give(a)
                st[h] = (s, a)

            def o_of(b, h, k):
                s, a = st[h]
                PE.wait([b.free, a, B[3][1], B[4][1]])
                bo = lambda t: b.v[:, (2 * k + t) * P:(2 * k + t + 1) * P]
                PE(lambda e: e.matmul(bo(0), s.v[:, 384:512], vof(h, 0), start=True, stop=True))
                PE(lambda e: e.matmul(bo(1), s.v[:, 512:640], vof(h, 0), start=True, stop=False))
                p = PE(lambda e: e.matmul(bo(1), s.v[:, 640:768], vof(h, 1), start=False, stop=True))
                s.give(p)
            for i in range(2):
                yield from prep(i)
                yield
            p2 = prep(2)
            next(p2)
            scores(0)
            yield
            yield
            run(p2)
            yield
            scores(1)
            combine(0)
            yield
            for h in range(2, 6):
                yield
                scores(h)
                combine(h - 1)
                yield
                turn(h - 2)
            yield
            combine(5)
            for i in range(3):
                qk[i].give((PE.sem, PE.n))
                bi[i].give((DV.sem, DV.n))
            turn(4)
            yield
            turn(5)
            yield
            out_banks(o_of, O, Otok, 0)
            out_banks(o_of, O, Otok, 1)
            yield
            out_banks(o_of, O, Otok, 2)
            yield

        if stop >= 3:
            xtok, xrs = norm(lambda t: X[:, t, :], g2, xs, None, acc, xt)
            B = {}
            O = [Slot(), Slot()]
            Otok = [[], []]
            Otok2 = [[], []]
            mk_ = mem_keys(mks, kvs[1], V("mk", 1))
            weave(u_block(1, 0, xtok), mk_, counts=(1, 1))
            df = diff(B, O, Otok)
            m2n, m2rs = norm(lambda t: mem_s[t].v, gm2, ys, m_tok)
            m2n.prep(0)
            m2n.prep(1)
            weave(u_block(1, 1), chain(take(df, 1), take(mk_, 2), take(df, 1)), counts=(1, 1, 1, 1))
            m2n.all()
            m2n.after()
            for t in range(2):
                mem_s[t].give((DV.sem, DV.n), (AC.sem, AC.n))
            weave(u_block(1, 2), df, counts=(1, 0, 0, 1))
            weave(u_block(1, 4), df, counts=(1, 1, 1, 1))
            qc1 = lambda t: B[4][0].v2[:, t, 256:512]
            ma = mem_attention(qc1, B[4][1], kT3(1), vv(1), [mks[1], kvs[1][1]], O, Otok2, V("mq", 1))

            def kv_block(i):
                box = []
                w = W["xattn_wv" if i > 1 else "xattn_wk"]
                for k, _ in enumerate(to_slot(block(w, 512 * (i % 2)), ys, m2n, box, m2rs)):
                    if k == 3:
                        s, tk = box[0]
                        tok = load(scr[i], s.v, tk, q=AC)
                        s.give(tok)
                        kv_out.append(tok)
                    yield
            weave(chain(u_block(1, 3), *(kv_block(i) for i in range(4))),
                  chain(take(df, 2), take(ma, 1), df, take(ma, 2), out_norm(O, Otok, 6, 128, 1.0 - LAMBDA_INIT, lambda t: (bm(R("subln"), 6), t_row)),
                        ma))
            xuse[id(xs)] = [(PE.sem, PE.n)]
            xuse[id(ys)] = [(PE.sem, PE.n)]
            fin = [(PE.sem, PE.n), (DV.sem, DV.n), (AC.sem, AC.n), (PO.sem, PO.n)]
            for i in (3, 4):
                B[i][0].give(*fin)
            kvs[1][0].give(*fin)
            g1 = get_gain("ffn1")
            acc = residual(W["w_out"][1], 8, xs, spread(lambda t, k: O[t].v[:, k * 512:(k + 1) * 512], xs,
                                                        lambda t, k: Otok[t] + Otok2[t]))
            for t in range(2):
                O[t].give((PE.sem, PE.n))
            xuse[id(xs)] = [(PE.sem, PE.n)]
        if stop >= 4:
            g2 = get_gain("mix2")
            acc = ffn(1, g1, acc)

        def softplus_terms(dst, src, n, tok):
            a = AC(lambda e: e.activation(dst, src, ACT.Abs), tok)
            a = AC(lambda e: e.activation(dst, dst, ACT.Exp, scale=-1.0), a)
            a = DV(lambda e: e.tensor_scalar(dst, dst, 1.0, None, ALU.add), a)
            return AC(lambda e: e.activation(dst, dst, ACT.Ln), a)

        def gdn_scalars(ga, tok, S):
            ab = ga[:, :, 0:8]
            z, sp_, g, be = (small(16).rearrange("p (t h) -> p t h", t=2) for _ in range(4))
            ea = small(8)
            a0 = AC(lambda e: e.activation(ea, R("a_log"), ACT.Exp), t_row)
            d = DV(lambda e: e.tensor_tensor(z, ab, bm(R("dt_bias"), 2), ALU.add), tok, t_row)
            l = softplus_terms(sp_, z, 16, d)
            d = DV(lambda e: e.scalar_tensor_tensor(sp_, z, 0.0, sp_, ALU.max, ALU.add), l)
            d = DV(lambda e: e.scalar_tensor_tensor(g, sp_, -1.0, bm(ea, 2), ALU.mult, ALU.mult), d, a0)
            a = AC(lambda e: e.activation(be, ga[:, :, 8:16], ACT.Exp, scale=-1.0), tok)
            db = DV(lambda e: e.tensor_scalar(be, be, 1.0, None, ALU.add), a)
            db = DV(lambda e: e.reciprocal(be, be), db)
            yield
            b = Bank()
            g2 = g.rearrange("p t h -> p (t h)")
            PE.wait([b.free, d, t_con2])
            PE(lambda e: e.matmul(b.v[:, 0:16], cU, g2, start=True, stop=True), sig=False)
            PE(lambda e: e.matmul(b.v[:, 16:32], cS, g2, start=True, stop=True), sig=False)
            for c in range(2):
                p = PE(lambda e: e.matmul(b.v[:, 32 + 16 * c:48 + 16 * c],
                                          con[:, 384 + 128 * c:512 + 128 * c], g2, start=True, stop=True))
            ex = small(64)
            a = AC(lambda e: e.activation(ex, b.v[:, 0:64], ACT.Exp), p)
            b.give(a)
            yield
            S["g"], S["beta"] = g, be
            S["egc"] = ex[:, 0:16].rearrange("p (t h) -> p t h", t=2)
            S["ekd"] = ex[:, 16:32].rearrange("p (t h) -> p t h", t=2)
            S["ge"] = ex[:, 32:64].rearrange("p (c t h) -> p c t h", c=2, t=2)
            S["tok"] = [a, db, d]

        def conv_half(z, f0, bx, rs_, wide):
            s, tk = bx
            y = Slot()
            yv = y.v.rearrange("p (f n) -> p f n", f=4)
            tks, ta = [], []
            th = Slot()

            def mul(fp):
                yh, hh = y.v[:, fp * 512:(fp + 1) * 512], th.v[:, fp * 512:(fp + 1) * 512]
                tks.append(DV(lambda e: e.scalar_tensor_tensor(yh, hh, 1.0, yh, ALU.add, ALU.mult), ta[fp]))
            for fp in range(2):
                b = Bank()
                PE.wait([b.free, tk])
                for f in range(2):
                    for t in range(2):
                        p = PE(lambda e: e.transpose(b.v[:, f * 256 + t * P:f * 256 + (t + 1) * P],
                                                     s.v2[:, t, (2 * fp + f) * P:(2 * fp + f + 1) * P], ident))
                for f in range(2):
                    cw = lambda n: V("conv", (f0 + 2 * fp + f) * 4 + n)
                    o = yv[:, 2 * fp + f, :]
                    bv = b.v[:, f * 256:(f + 1) * 256]
                    a = AC(lambda e: e.mul(o, bv, cw(3)), p, y.free, t_vec)
                for f in range(2):
                    cw = lambda n: V("conv", (f0 + 2 * fp + f) * 4 + n)
                    o = yv[:, 2 * fp + f, :]
                    bv = b.v[:, f * 256:(f + 1) * 256]
                    d = a
                    for n in (2, 1, 0):
                        sh = 3 - n
                        d = DV(lambda e: e.scalar_tensor_tensor(o[:, sh:256], bv[:, 0:256 - sh], cw(n), o[:, sh:256],
                                                                ALU.mult, ALU.add), d)
                b.give(d)
                yh, hh = y.v[:, fp * 512:(fp + 1) * 512], th.v[:, fp * 512:(fp + 1) * 512]
                ta.append(AC(lambda e: e.activation(hh, yh, ACT.Tanh, scale=0.5), d, th.free))
                if fp == 1:
                    mul(0)
                yield
            mul(1)
            th.give(tks[1])
            if wide:
                yield
            nt = []
            for t in range(2):
                b = Bank()
                PE.wait([b.free, tks])
                for f in range(4):
                    p = PE(lambda e: e.transpose(b.v[:, f * P:(f + 1) * P], yv[:, f, t * P:(t + 1) * P], ident))
                a = AC(lambda e: e.copy(s.v2[:, t, :], b.v), p)
                b.give(a)
                nt.append(a)
            y.give(p)
            bx[1] = nt
            if z < 2:
                rs_.append(group_rs(s.v, 8, P, 0.25, EPS, nt))
            yield

        def gdn_mid(hf, box, S, sc, G_):
            (qs, qtk), (ks, ktk), (vs, vtk) = box
            hs = slice(4 * hf, 4 * hf + 4)
            th8 = lambda a: a.rearrange("p (t h) -> p t h", t=2)
            rq, rk = th8(sc[0][0]), th8(sc[1][0])
            cq, cqd, ck, ckb, crk, ckd, cv = (small(8).rearrange("p (t h) -> p t h", t=2) for _ in range(7))
            d = DV(lambda e: e.tensor_scalar(cq, rq, 0.5 * P ** -0.5, None, ALU.mult), sc[0][1])
            tqd = DV(lambda e: e.tensor_tensor(cqd, cq, S["egc"][:, :, hs], ALU.mult), d, S["tok"])
            d = DV(lambda e: e.tensor_scalar(ck, rk, 0.5, None, ALU.mult), sc[1][1])
            d2 = DV(lambda e: e.tensor_tensor(ckb, ck, S["beta"][:, :, hs], ALU.mult), d)
            DV(lambda e: e.tensor_tensor(ckd, ck, S["ekd"][:, :, hs], ALU.mult), d)
            DV(lambda e: e.tensor_tensor(crk, ckb, S["egc"][:, :, hs], ALU.mult), d2)
            tcf = DV(lambda e: e.tensor_scalar(cv, S["beta"][:, :, hs], 0.5, None, ALU.mult), S["tok"])
            h4 = lambda a: a.rearrange("p (h n) -> p h n", h=4)
            dec = Slot()
            gU = Slot()
            dt_ = []
            gm = []
            for t in range(2):
                gv = h4(gU.v2[:, t, :])
                gm.append(PO(lambda e: e.tensor_tensor(gv, bm(cU, 4), bc(S["g"][:, t, hs], P), ALU.mult), S["tok"], gU.free))
            for t in range(2):
                m = gm[t]
                b = Bank()
                p = PE(lambda e: e.matmul(b.v, cS, gU.v2[:, t, :], start=True, stop=True), m, b.free)
                dv = dec.v2[:, t, :]
                a = AC(lambda e: e.activation(dv, b.v, ACT.Exp), p, dec.free)
                b.give(a)
                dt_.append(PO(lambda e: e.tensor_tensor(h4(dv), h4(dv), bm(cU, 4), ALU.mult), a))
            gU.give(p)
            kT = Slot()
            lq = [Slot(), Slot()]
            qd = Slot()
            rkS = Slot()
            rt_ = PO(lambda e: e.tensor_tensor(rkS.v.rearrange("p (a n) -> p a n", n=P),
                                               ks.v.rearrange("p (a n) -> p a n", n=P),
                                               bc(crk.rearrange("p t h -> p (t h)"), P), ALU.mult),
                     tcf, ktk, rkS.free)
            kTt, lqt, qdt = [], [[], []], []
            for t in range(2):
                for c, src, stk, dst, fr, lst in (
                        (ck, ks, ktk, h4(kT.v2[:, t, :]), kT.free, kTt),
                        (ckb, ks, ktk, lq[t].v.rearrange("p (h l n) -> p h l n", h=4, l=2)[:, :, 0, :], lq[t].free, lqt[t]),
                        (cq, qs, qtk, lq[t].v.rearrange("p (h l n) -> p h l n", h=4, l=2)[:, :, 1, :], lq[t].free, lqt[t]),
                        (cqd, qs, qtk, h4(qd.v2[:, t, :]), qd.free, qdt)):
                    tmp = Slot()
                    m = DV(lambda e: e.tensor_tensor(h4(tmp.v[:, 0:512]), h4(src.v2[:, t, :]), bc(c[:, t, :], P),
                                                     ALU.mult), tcf, stk, tmp.free, tqd)
                    b = Bank()
                    PE.wait([b.free, m])
                    for h in range(4):
                        p = PE(lambda e: e.transpose(b.v[:, h * P:(h + 1) * P], tmp.v[:, h * P:(h + 1) * P], ident))
                    a = AC(lambda e: e.copy(dst, b.g(4)), p, fr)
                    b.give(a)
                    tmp.give(p)
                    lst.append(a)
                yield
            qs.give((DV.sem, DV.n))
            k3 = ks.v.rearrange("p (a n) -> p a n", n=P)
            kdt = DV(lambda e: e.tensor_tensor(k3, k3, bc(ckd.rearrange("p t h -> p (t h)"), P), ALU.mult), rt_, kTt, lqt)
            v3 = vs.v.rearrange("p (a n) -> p a n", n=P)
            rvt = PO(lambda e: e.tensor_tensor(v3, v3, bc(cv.rearrange("p t h -> p (t h)"), P), ALU.mult), tcf, vtk)
            la = [Slot(), Slot()]
            lat = [[], []]
            for t in range(2):
                for hp in range(2):
                    b = Bank()
                    PE.wait([b.free, kTt[t], lqt[t]])
                    for k in range(2):
                        h = 2 * hp + k
                        p = PE(lambda e: e.matmul(b.v[:, k * 256:(k + 1) * 256], kT.v2[:, t, h * P:(h + 1) * P],
                                                  lq[t].v[:, h * 256:(h + 1) * 256], start=True, stop=True))
                    o = la[t].v[:, hp * 512:(hp + 1) * 512].rearrange("p (h l n) -> p h l n", h=2, l=2)
                    bv = b.v.rearrange("p (h l n) -> p h l n", h=2, l=2)
                    dd = h4(dec.v2[:, t, :])[:, 2 * hp:2 * hp + 2, :]
                    for l in range(2):
                        d = DV(lambda e: e.tensor_tensor(o[:, :, l, :], bv[:, :, l, :], dd, ALU.mult), p, dt_[t], la[t].free)
                    b.give(d)
                    lat[t].append(d)
                lq[t].give(p)
                yield
            kT.give((PE.sem, PE.n))
            dec.give((DV.sem, DV.n))
            M, N, Tt, Cm = Slot(), Slot(), Slot(), Slot()
            LT = lambda t: la[t].v.rearrange("p (h l n) -> p h l n", h=4, l=2)[:, :, 0, :]
            AT = lambda t, h: la[t].v[:, h * 256 + P:h * 256 + 2 * P]
            mt, nt_, ct = [None, None], [None, None], [None, None]
            idb = bm(ident, 4)
            cfree = [list(Cm.free), list(Cm.free)]
            tfree = [list(Tt.free), list(Tt.free)]
            for lv in range(6):
                mask = bm(con[:, 640 + P * lv:768 + P * lv], 4)
                for t in range(2):
                    cv_ = h4(Cm.v2[:, t, :])
                    ct[t] = PO(lambda e: e.tensor_tensor(cv_, LT(t), mask, ALU.mult), lat[t], cfree[t])
                for t in range(2):
                    b = Bank()
                    PE.wait([b.free, ct[t], mt[t], nt_[t]])
                    for h in range(4):
                        hh = slice(h * P, (h + 1) * P)
                        if lv == 0:
                            p = PE(lambda e: e.transpose(b.v[:, hh], Cm.v2[:, t, hh], ident))
                        else:
                            p = PE(lambda e: e.matmul(b.v[:, hh], Cm.v2[:, t, hh], M.v2[:, t, hh], start=True, stop=True))
                    if lv == 0:
                        mt[t] = DV(lambda e: e.scalar_tensor_tensor(h4(M.v2[:, t, :]), b.g(4), -1.0, idb,
                                                                    ALU.mult, ALU.add), p, M.free)
                        b.give(mt[t])
                        nt_[t] = DV(lambda e: e.scalar_tensor_tensor(h4(N.v2[:, t, :]), h4(Cm.v2[:, t, :]), -1.0, idb,
                                                                     ALU.mult, ALU.add), ct[t], N.free)
                        cfree[t] = [nt_[t], p]
                        continue
                    cfree[t] = [p]
                    tt = AC(lambda e: e.copy(Tt.v2[:, t, :], b.v), p, tfree[t])
                    b.give(tt)
                    tfree[t] = tt
                if lv == 0:
                    yield
                    continue
                for t in range(2):
                    bM = Bank() if lv < 5 else None
                    bN = Bank()
                    PE.wait([tfree[t], bN.free, bM.free if bM else None])
                    if bM:
                        for h in range(4):
                            hh = slice(h * P, (h + 1) * P)
                            p1 = PE(lambda e: e.matmul(bM.v[:, hh], N.v2[:, t, hh], Tt.v2[:, t, hh], start=True, stop=True))
                    for h in range(4):
                        hh = slice(h * P, (h + 1) * P)
                        p = PE(lambda e: e.matmul(bN.v[:, hh], Tt.v2[:, t, hh], N.v2[:, t, hh], start=True, stop=True))
                    if bM:
                        mt[t] = DV(lambda e: e.scalar_tensor_tensor(M.v2[:, t, :], bM.v, -1.0, M.v2[:, t, :],
                                                                    ALU.mult, ALU.add), p1)
                        bM.give(mt[t])
                    nt_[t] = DV(lambda e: e.scalar_tensor_tensor(N.v2[:, t, :], bN.v, -1.0, N.v2[:, t, :],
                                                                 ALU.mult, ALU.add), p)
                    bN.give(nt_[t])
                    tfree[t] = [p]
                yield
            last = [(PE.sem, PE.n), (DV.sem, DV.n), (PO.sem, PO.n)]
            M.give(*last)
            Tt.give(*last)
            Cm.give(*last)
            us, wT = Slot(), Slot()
            ut, wt = [], []
            for t in range(2):
                b = Bank()
                PE.wait([b.free, nt_[t], rvt])
                for h in range(4):
                    hh = slice(h * P, (h + 1) * P)
                    p = PE(lambda e: e.matmul(b.v[:, hh], N.v2[:, t, hh], vs.v2[:, t, hh], start=True, stop=True))
                a = AC(lambda e: e.copy(us.v2[:, t, :], b.v), p, us.free)
                b.give(a)
                ut.append(a)
                b = Bank()
                PE.wait([b.free, rt_])
                for h in range(4):
                    hh = slice(h * P, (h + 1) * P)
                    p = PE(lambda e: e.matmul(b.v[:, hh], rkS.v2[:, t, hh], N.v2[:, t, hh], start=True, stop=True))
                a = AC(lambda e: e.copy(wT.v2[:, t, :], b.v), p, wT.free)
                b.give(a)
                wt.append(a)
            N.give(p)
            rkS.give(p)
            yield
            G_.update(us=us, wT=wT, ut=ut, wt=wt, ks=ks, vs=vs, kdt=kdt, qd=qd, qdt=qdt, la=la, lat=lat, AT=AT)

        def gdn_scan(hf, S, G_, res):
            us, wT, ut, wt, ks, kdt, qd, qdt, la, lat, AT = (G_[n] for n in (
                "us", "wT", "ut", "wt", "ks", "kdt", "qd", "qdt", "la", "lat", "AT"))
            hs = slice(4 * hf, 4 * hf + 4)
            h4 = lambda a: a.rearrange("p (h n) -> p h n", h=4)
            St = Slot()
            stok = None
            ot = []
            sfree = [list(St.free), list(St.free)]
            oslot = Slot()
            for c in range(4):
                t, p0 = c // 2, 64 * (c % 2)
                rows = slice(p0, p0 + 64)
                sv, nv = St.v2[:, (c + 1) % 2, :], St.v2[:, c % 2, :]
                dl = us.v2[rows, t, :]
                dtok = ut[t]
                if 0 < c < 3:
                    m = PO(lambda e: e.tensor_tensor(h4(nv), h4(sv), bc(S["ge"][:, c % 2, t, hs], P), ALU.mult),
                           stok, sfree[c % 2])
                if c:
                    b = Bank()
                    PE.wait([b.free, wt[t], stok])
                    for h in range(4):
                        p = PE(lambda e: e.matmul(b.v[rows, h * P:(h + 1) * P], wT.v2[:, t, h * P + p0:h * P + p0 + 64],
                                                  sv[:, h * P:(h + 1) * P], start=True, stop=True))
                    dtok = DV(lambda e: e.scalar_tensor_tensor(dl, b.v[rows, :], -1.0, dl, ALU.mult, ALU.add), p, ut[t])
                    b.give(dtok)
                    yield
                if c < 3:
                    b = Bank()
                    PE.wait([b.free, dtok, kdt])
                    for h in range(4):
                        hh = slice(h * P, (h + 1) * P)
                        p = PE(lambda e: e.matmul(b.v[:, hh], ks.v2[rows, t, hh], us.v2[rows, t, hh], start=True, stop=True))
                    if c == 0:
                        stok = DV(lambda e: e.tensor_copy(nv, b.v), p, sfree[0])
                    else:
                        stok = DV(lambda e: e.tensor_tensor(nv, b.v, nv, ALU.add), p, m)
                    b.give(stok)
                b = Bank()
                PE.wait([b.free, dtok, qdt[t], lat[t]])
                for h in range(4):
                    hh = slice(h * P, (h + 1) * P)
                    if c:
                        PE(lambda e: e.matmul(b.v[rows, hh], qd.v2[:, t, h * P + p0:h * P + p0 + 64], sv[:, hh],
                                              start=True, stop=False), sig=False)
                    p = PE(lambda e: e.matmul(b.v[rows, hh], AT(t, h)[rows, p0:p0 + 64], us.v2[rows, t, hh],
                                              start=(c == 0), stop=True))
                sfree[(c + 1) % 2] = [p, m] if 0 < c < 3 else [p]
                a = AC(lambda e: e.copy(oslot.v2[rows, t, :], b.v[rows, :]), p, oslot.free)
                b.give(a)
                ot.append(a)
                yield
            end = [(PE.sem, PE.n), (DV.sem, DV.n), (AC.sem, AC.n), (PO.sem, PO.n)]
            for s_ in (ks, G_["vs"], us, wT, St, qd, la[0], la[1]):
                s_.give(*end)
            res.append((oslot, ot))
            yield

        def gla(box, ga, gtok, tg, res):
            (qs, qtk), (ks, ktk) = box[0], box[1]
            qT, kT = Slot(), Slot()
            tt = [[], []]
            for w, (s_, tk, dst, sc_) in enumerate(((qs, qtk, qT, P ** -0.5), (ks, ktk, kT, 1.0))):
                for hp in range(2):
                    b = Bank()
                    PE.wait([b.free, tk])
                    for k in range(2):
                        for t in range(2):
                            p = PE(lambda e: e.transpose(b.v[:, k * 256 + t * P:k * 256 + (t + 1) * P],
                                                         s_.v2[:, t, (2 * hp + k) * P:(2 * hp + k + 1) * P], ident))
                    a = AC(lambda e: e.mul(dst.v[:, hp * 512:(hp + 1) * 512], b.v, sc_), p, dst.free)
                    b.give(a)
                    tt[w].append(a)
            qs.give(p)
            ks.give(p)
            yield
            reset = Slot()
            m = PO(lambda e: e.memset(reset.v, 1.0), reset.free)
            rv = reset.v.rearrange("p (a n) -> p a n", n=64)
            m = PO(lambda e: e.memset(rv[:, :, 0:1], 0.0), m)
            b = Bank()
            PE.wait([b.free, gtok, t_con])
            for t in range(2):
                p = PE(lambda e: e.transpose(b.v[0:16, t * P:(t + 1) * P], ga[:, t, 16:32], ident))
            lg = Slot()
            a = AC(lambda e: e.copy(lg.v[0:16, 0:256], b.v[0:16, 0:256]), p, lg.free)
            b.give(a)
            yield
            z = Slot()
            zt = []
            for hp in range(2):
                b = Bank()
                PE.wait([b.free, a, tg])
                for k in range(2):
                    h = 2 * hp + k
                    p = PE(lambda e: e.matmul(b.v[:, k * 256:(k + 1) * 256], gl2[:, h * P:(h + 1) * P],
                                              lg.v[0:16, 0:256], start=True, stop=True))
                for k in range(2):
                    h = 2 * hp + k
                    d = DV(lambda e: e.tensor_scalar(z.v[:, h * 256:(h + 1) * 256], b.v[:, k * 256:(k + 1) * 256],
                                                     V("b_gate", h), None, ALU.add), p, z.free, t_vec)
                b.give(d)
                zt.append(d)
            lg.give(p)
            yield
            l = Slot()
            d = AC(lambda e: e.activation(l.v, z.v, ACT.Abs), zt, l.free)
            d = AC(lambda e: e.activation(l.v, l.v, ACT.Exp, scale=-1.0), d)
            d = DV(lambda e: e.tensor_scalar(l.v, l.v, 1.0, None, ALU.add), d)
            yield
            d = AC(lambda e: e.activation(l.v, l.v, ACT.Ln), d)
            d = DV(lambda e: e.scalar_tensor_tensor(l.v, z.v, 0.0, l.v, ALU.min, ALU.subtract), d)
            bcum = z
            d = DV(lambda e: e.tensor_tensor_scan(bcum.v, reset.v, l.v, 0.0, ALU.mult, ALU.add), d, m)
            reset.give(d)
            yield
            yield
            b64 = bcum.v.rearrange("p (a n) -> p a n", n=64)
            e4, e1, e2 = Slot(), l, Slot()
            v64 = lambda s: s.v.rearrange("p (a n) -> p a n", n=64)
            dr = DV(lambda e: e.tensor_tensor(v64(e1), b64, b64[:, :, 32:33].to_broadcast([P, 16, 64]), ALU.subtract), d)
            dl = DV(lambda e: e.tensor_tensor(v64(e4), b64[:, :, 63:64].to_broadcast([P, 16, 64]), b64, ALU.subtract),
                    d, e4.free)
            gend = small(16)
            tau = 1.0 / 16.0
            ag = AC(lambda e: e.activation(gend.unsqueeze(2), b64[:, :, 63:64], ACT.Exp, scale=tau), d)
            a2 = AC(lambda e: e.activation(e2.v, e1.v, ACT.Exp, scale=-tau), dr, e2.free)
            a1 = AC(lambda e: e.activation(e1.v, e1.v, ACT.Exp, scale=tau), a2)
            a4 = AC(lambda e: e.activation(e4.v, e4.v, ACT.Exp, scale=tau), dl)
            a3 = AC(lambda e: e.activation(bcum.v, bcum.v, ACT.Exp, scale=tau), dl, ag)
            q1 = DV(lambda e: e.tensor_tensor(e1.v, e1.v, qT.v, ALU.mult), a1, tt[0])
            k2 = DV(lambda e: e.tensor_tensor(e2.v, e2.v, kT.v, ALU.mult), a2, tt[1])
            q3 = PO(lambda e: e.tensor_tensor(bcum.v, bcum.v, qT.v, ALU.mult), a3, tt[0])
            yield
            k4 = DV(lambda e: e.tensor_tensor(e4.v, e4.v, kT.v, ALU.mult), a4, tt[1])
            yield
            qT.give(q1, q3)
            kT.give(k2, k4)
            at = Slot()
            att = []
            for t in range(2):
                b = Bank()
                PE.wait([b.free, q1, k2])
                for h in range(4):
                    cc = slice(h * 256 + t * P, h * 256 + (t + 1) * P)
                    p = PE(lambda e: e.matmul(b.v[:, h * P:(h + 1) * P], e2.v[:, cc], e1.v[:, cc], start=True, stop=True))
                a = AC(lambda e: e.copy(at.v2[:, t, :], b.v), p, at.free)
                b.give(a)
                av = at.v2[:, t, :].rearrange("p (h n) -> p h n", h=4)
                att.append(PO(lambda e: e.affine_select(out=av, in_=av, pattern=[[0, 4], [1, P]], compare_op=ALU.is_ge,
                                                        fill=0.0, base=0, channel_multiplier=-1), a))
            e1.give(p)
            e2.give(p)
            yield
            kd = Slot()
            kdt = []
            for t in range(2):
                b = Bank()
                PE.wait([b.free, k4])
                for h in range(4):
                    p = PE(lambda e: e.transpose(b.v[:, h * P:(h + 1) * P], e4.v[:, h * 256 + t * P:h * 256 + (t + 1) * P], ident))
                a = AC(lambda e: e.copy(kd.v2[:, t, :], b.v), p, kd.free)
                b.give(a)
                kdt.append(a)
            e4.give(p)
            yield
            vsl = lambda h: box[2 + h // 2][0].v2[:, :, (h % 2) * 256:(h % 2 + 1) * 256]
            vtok = [box[2][1], box[3][1]]
            Sts = [Slot(), Slot()]
            sfree = [list(Sts[0].free), list(Sts[1].free)]
            stok = None
            oo = [Slot(), Slot()]
            ot = [[], []]
            for c in range(4):
                t, p0 = c // 2, 64 * (c % 2)
                rows = slice(p0, p0 + 64)
                kb_ = []
                St, Sn = Sts[(c + 1) % 2], Sts[c % 2]
                s4 = lambda S_: S_.v.rearrange("p (h n) -> p h n", h=4)
                if 0 < c < 3:
                    gv = gend.rearrange("p (h c) -> p h c", c=4)[:, :, c]
                    m = PO(lambda e: e.tensor_tensor(s4(Sn), s4(St), bc(gv, 256), ALU.mult), stok, sfree[c % 2])
                if c < 3:
                    for hp in range(2):
                        b = Bank()
                        PE.wait([b.free, kdt, vtok])
                        for k in range(2):
                            h = 2 * hp + k
                            p = PE(lambda e: e.matmul(b.v[:, k * 256:(k + 1) * 256], kd.v2[rows, t, h * P:(h + 1) * P],
                                                      vsl(h)[rows, t, :], start=True, stop=True))
                        s2 = Sn.v[:, hp * 512:(hp + 1) * 512]
                        if c == 0:
                            d = DV(lambda e: e.tensor_copy(s2, b.v), p, sfree[0])
                        else:
                            d = DV(lambda e: e.tensor_tensor(s2, b.v, s2, ALU.add), p, m)
                        b.give(d)
                        kb_.append(d)
                for hp in range(2):
                    b = Bank()
                    PE.wait([b.free, att[t], q3, stok, vtok])
                    for k in range(2):
                        h = 2 * hp + k
                        bo = b.v[rows, k * 256:(k + 1) * 256]
                        if c:
                            PE(lambda e: e.matmul(bo, bcum.v[:, h * 256 + c * 64:h * 256 + c * 64 + 64],
                                                  St.v[:, h * 256:(h + 1) * 256], start=True, stop=False), sig=False)
                        p = PE(lambda e: e.matmul(bo, at.v2[rows, t, h * P + p0:h * P + p0 + 64], vsl(h)[rows, t, :],
                                                  start=(c == 0), stop=True))
                    a = AC(lambda e: e.copy(oo[t].v[rows, hp * 512:(hp + 1) * 512], b.v[rows, :]), p, oo[t].free)
                    b.give(a)
                    ot[t].append(a)
                sfree[(c + 1) % 2] = [p, m] if 0 < c < 3 else [p]
                stok = kb_
                yield
            end = [(PE.sem, PE.n), (DV.sem, DV.n), (AC.sem, AC.n), (PO.sem, PO.n)]
            for s_ in (bcum, kd, at, Sts[0], Sts[1], box[2][0], box[3][0]):
                s_.give(*end)
            res.append((oo, ot))

        if stop >= 5:
            xtok, xrs = norm(lambda t: X[:, t, :], g2, xs, None, acc, xt)
            W2 = W["w_in_2"]
            ga = Slot()
            gav = ga.v[:, 0:64].rearrange("p (t n) -> p t n", t=2)
            w3 = W2.rearrange("(k p) n -> p k n", p=P)
            t1 = load(sraw[:, :, 0:16], w3[:, :, 4096:4112])
            t2 = load(sraw[:, :, 16:32], w3[:, :, 7184:7200])
            a = AC(lambda e: e.copy(sspl[:, 0], sraw[:, :, :]), t1, t2)
            d = DV(lambda e: e.tensor_tensor(sspl[:, 1], sraw[:, :, :], sspl[:, 0].bitcast(F32), ALU.subtract), a)
            small_done = d
            S = {}

            def narrow():
                b = Bank()
                PE.wait([b.free, small_done] + list(xtok.tok.values()))
                for t in range(2):
                    for k in range(8):
                        for n, (l, m) in enumerate(((0, 0), (0, 1), (1, 0))):
                            p = PE(lambda e: e.matmul(b.v[:, t * 32:(t + 1) * 32], xs[:, l, k, t * P:(t + 1) * P],
                                                      sspl[:, m, k, :], start=(k == 0 and n == 0),
                                                      stop=(k == 7 and n == 2)))
                for t in range(2):
                    a = AC(lambda e: e.mul(gav[:, t, :], b.v[:, t * 32:(t + 1) * 32], xrs[t][0]), p, ga.free, xrs[t][1])
                b.give(a)
                gtok.append(a)
                yield
                yield from gdn_scalars(gav, gtok, S)
            gtok = []
            BA, BB, GL, Z, G = {}, {}, {}, {}, {}
            ho, go = [], []
            rsA, rsB, GA, GB = [], [], {}, {}

            tg = load(gl2[:, :], W["gate2"])

            def blk(c, D_, i, tile_rs=None, pre=None):
                return to_slot(block(W2, c), xs, xtok, (D_, i), tile_rs or xrs, FIRST if pre else (1,) * 4, pre)

            def gate_blk(i):
                s = Slot()

                def done(b, toks):
                    tk = []
                    for t in range(2):
                        a = AC(lambda e: e.activation(s.v2[:, t, :], b[t].v, ACT.Tanh, scale=hrs[t][0]), toks[t],
                               s.free, hrs[t][1])
                        b[t].give(a)
                        tk.append(a)
                    G[i] = (s, tk)
                yield from cols(block(W2, 7200 + 512 * i), xs, xtok, done)

            def conv(z, hf, D_, rs_):
                D_[z] = list(D_[z])
                yield from conv_half(z, 8 * z + 4 * hf, D_[z], rs_, True)

            def out_gdn():
                rr = [group_rs(ho[hf][0].v, 8, P, 1.0 / P, EPS, ho[hf][1], 0.25) for hf in range(2)]
                yield
                for hf in range(2):
                    s = ho[hf][0]
                    o8 = s.v.rearrange("p (a n) -> p a n", n=P)
                    d1 = DV(lambda e: e.tensor_tensor(o8, o8, bc(rr[hf][0], P), ALU.mult), rr[hf][1])
                    d1 = DV(lambda e: e.tensor_tensor(s.v, s.v, Z[hf][0].v, ALU.mult), d1, zt[hf])
                    Z[hf][0].give(d1)
                    ya.append(d1)
                    yield
            ya, zt = [], {}

            def gates_in(k, g):
                s, tk = Z[k]
                th = Slot()
                a = AC(lambda e: e.activation(th.v, s.v, ACT.Tanh, scale=0.5), tk, th.free)
                yield
                d = DV(lambda e: e.scalar_tensor_tensor(s.v, th.v, 1.0, s.v, ALU.add, ALU.mult), a)
                th.give(d)
                v3 = s.v.rearrange("p (a n) -> p a n", a=g.shape[1])
                zt[k] = PO(lambda e: e.tensor_tensor(v3, v3, g, ALU.mult), d, t_row)
                yield
            g_gdn, g_gla = bm(R("gdn_g"), 8), bm(R("gla_g"), 4)
            nw = narrow()
            weave(blk(0, BA, 0, None, xtok), nw, counts=(1, 1))
            hrs = []
            for t in range(2):
                h_ = small(1)
                hrs.append((h_, DV(lambda e: e.tensor_scalar(h_, xrs[t][0], 0.5, None, ALU.mult), xrs[t][1])))
            weave(blk(1024, BA, 1), both(conv(0, 0, BA, rsA), nw), 2)
            weave(blk(2048, BA, 2), conv(1, 0, BA, rsA))

            def mid_a():
                yield from conv(2, 0, BA, rsA)
                yield from gdn_mid(0, [BA[z] for z in range(3)], S, rsA, GA)
            weave(chain(blk(512, BB, 0), blk(1536, BB, 1), blk(2560, BB, 2)), mid_a())
            bg = both(gdn_scan(0, S, GA, ho), chain(*(conv(z, 1, BB, rsB) for z in range(3))))
            weave(chain(blk(4112, GL, 0), blk(4624, GL, 1), blk(5136, GL, 2)), bg, counts=(2,) * 8 + (1,) * 4)
            run(bg)
            weave(chain(blk(5648, GL, 3), blk(3072, Z, 0)),
                  gdn_mid(1, [BB[z] for z in range(3)], S, rsB, GB))
            zs = chain(gates_in(0, g_gdn), gates_in(1, g_gdn))
            gs_ = gdn_scan(1, S, GB, ho)
            bg = both(gs_, chain(iter([0] * 2), zs))
            weave(blk(3584, Z, 1), bg, counts=(1, 2, 2, 1))
            weave(blk(6160, Z, 2), bg, 2)
            gl = gla([GL[i] for i in range(4)], gav, gtok, tg, go)
            bg = both(out_gdn(), gl)
            weave(chain(blk(6672, Z, 3), gate_blk(0)), bg, counts=(1,) * 8)
            yat = spread(lambda t, k: ho[k][0].v2[:, t, :], ys, lambda t, k: ya[k])
            yat.all()
            for hf in range(2):
                ho[hf][0].give((PE.sem, PE.n))
            weave(chain(*(gate_blk(i) for i in range(1, 4))), both(bg, chain(iter([0] * 4), gates_in(2, g_gla), gates_in(3, g_gla))), 2)
            xuse[id(xs)] = [(PE.sem, PE.n)]
            ga.give((DV.sem, DV.n), (PE.sem, PE.n))

            def merged(w, xin_, xtok_, gs, prev, box, pre=None, groups=None):
                acc = [[Bank(), Bank()], [Bank(), Bank()]]
                tht = [gs[j][1] for j in range(2)]
                for toks in rows_(w, range(8), xin_, 0, xtok_, acc, True, True, groups, pre):
                    yield
                dd = [[], []]
                for j in range(2):
                    s, tk = gs[j]
                    box.append((s, dd[j]))
                for t in range(2):
                    for j in range(2):
                        s, tk = gs[j]
                        v = s.v2[:, t, :]
                        if prev is not None:
                            v0 = prev[j][0].v2[:, t, :]
                        d = DV(lambda e: e.scalar_tensor_tensor(v, v, 1.0, acc[t][j].v, ALU.add, ALU.mult), tht[j], toks[t])
                        acc[t][j].give(d)
                        if prev is not None:
                            d = DV(lambda e: e.tensor_tensor(v, v, v0, ALU.add), d, prev[j][1])
                        dd[j].append(d)
                if prev is not None:
                    for j in range(2):
                        prev[j][0].give(d)

            (oo, ot) = go[0]

            def out_gla():
                rr = [group_rs(oo[t].v, 4, 256, 1.0 / 256, EPS, ot[t], 0.25) for t in range(2)]
                yield
                for t in range(2):
                    s = oo[t]
                    o4 = s.v.rearrange("p (a n) -> p a n", n=256)
                    d1 = DV(lambda e: e.tensor_tensor(o4, o4, bc(rr[t][0], 256), ALU.mult), rr[t][1])
                    for hf in range(2):
                        sv = s.v[:, hf * 512:(hf + 1) * 512]
                        zv = Z[2 + hf][0].v2[:, t, :]
                        d2 = DV(lambda e: e.tensor_tensor(sv, sv, zv, ALU.mult), d1, zt[2 + hf])
                    yb.append(d2)
                    yield
                for hf in range(2):
                    Z[2 + hf][0].give(d2)
            lr, yb = [], []
            m1, m2 = [], []
            weave(merged(W["w_branch_gdn"], ys, yat, [G[0], G[1]], None, m1), out_gla())
            xuse[id(ys)] = [(PE.sem, PE.n)]
            ybt = spread(lambda t, k: oo[t].v[:, k * 512:(k + 1) * 512], xs, lambda t, k: yb[t])
            run(merged(W["w_branch_gla"], xs, ybt, [G[2], G[3]], m1, m2, ybt, (3, 1, 1, 3)))
            for t in range(2):
                oo[t].give((PE.sem, PE.n))
            xuse[id(xs)] = [(PE.sem, PE.n)]
            gxa = get_gain("xattn")
            kv_in = []
            for i in range(4):
                s_ = Slot()
                tok = load(s_.v, scr[i], s_.free, kv_out[i])
                kv_in.append((s_, [tok, tok]))
            acc = residual(W["w_out_2"], 8, ys, spread(lambda t, j: m2[j][0].v2[:, t, :], ys, lambda t, j: m2[j][1][t]))
            for j in range(2):
                m2[j][0].give((PE.sem, PE.n))
            xuse[id(ys)] = [(PE.sem, PE.n)]

        if stop >= 6:
            K, Vv, Q = kv_in[0:2], kv_in[2:4], []
            xn, xrs = norm(lambda t: X[:, t, :], gxa, xs, None, acc, xt)
            kT = [Slot(), Slot()]

            def turn_feat(B_, dst, scale, toks):
                for i in range(2):
                    s, tk = B_[i]
                    for fp in range(2):
                        b = Bank()
                        PE.wait([b.free, tk])
                        for f in range(2):
                            for t in range(2):
                                p = PE(lambda e: e.transpose(b.v[:, f * 256 + t * P:f * 256 + (t + 1) * P],
                                                             s.v2[:, t, (2 * fp + f) * P:(2 * fp + f + 1) * P], ident))
                        a = AC(lambda e: e.mul(dst[i].v[:, fp * 512:(fp + 1) * 512], b.v, scale), p, dst[i].free)
                        b.give(a)
                        toks.append(a)
                    s.give(p)
                    yield
            ktk, qtk = [], []
            tK = turn_feat(K, kT, 1.0, ktk)
            run(to_slot(block(W["xattn_wq"], 0), xs, xn, Q, xrs, FIRST, xn))
            weave(to_slot(block(W["xattn_wq"], 512), xs, xn, Q, xrs), tK)
            xuse[id(xs)] = [(PE.sem, PE.n)]
            qT = [Slot(), Slot()]
            run(turn_feat(Q, qT, 1.0 / 16.0, qtk))
            gm = get_gain("mlp")
            ftT = lambda s, f: s[f // 4].v[:, (f % 4) * 256:(f % 4 + 1) * 256]
            wTs = []

            def xat(t):
                sc, st_ = [], []
                for hp in range(2):
                    b = Bank()
                    PE.wait([b.free, qtk, ktk])
                    for k in range(2):
                        h = 2 * hp + k
                        for f in range(2):
                            p = PE(lambda e: e.matmul(b.v[:, k * 256:(k + 1) * 256],
                                                      ftT(qT, 2 * h + f)[:, t * P:(t + 1) * P], ftT(kT, 2 * h + f),
                                                      start=(f == 0), stop=(f == 1)))
                    sc.append(b)
                    st_.append(p)
                w, wtok, _, _ = softmax_mem(t, sc, st_, True)
                yield
                wT = Slot()
                tt = transposed8(w.v, wtok, wT.v, wT.free)
                w.give((PE.sem, PE.n))
                wTs.append((wT, tt))
                yield
            g0, g1_ = xat(0), xat(1)
            next(g0)
            next(g1_)
            run(g0)
            run(g1_)
            oxt = []
            for h in range(4):
                b = Bank()
                vs_ = Vv[h // 2]
                PE.wait([b.free, wTs[0][1], wTs[1][1], vs_[1]])
                for f in range(2):
                    for t in range(2):
                        for m in range(2):
                            p = PE(lambda e: e.matmul(b.v[:, f * 256 + t * P:f * 256 + (t + 1) * P],
                                                      vs_[0].v2[:, m, (h % 2) * 256 + f * P:(h % 2) * 256 + (f + 1) * P],
                                                      wTs[t][0].v[:, (2 * h + m) * P:(2 * h + m + 1) * P],
                                                      start=(m == 0), stop=(m == 1)))
                o = lambda l_: ys[:, l_, 2 * h:2 * h + 2, :]
                a = AC(lambda e: e.copy(o(0), b.g(2)), p, *xuse[id(ys)])
                d = DV(lambda e: e.tensor_tensor(o(1), b.g(2), o(0).bitcast(F32), ALU.subtract), a)
                b.give(d)
                oxt.append(d)
            for s_ in (qT + kT + [Vv[0][0], Vv[1][0], wTs[0][0], wTs[1][0]]):
                s_.give((PE.sem, PE.n))
            acc = [[Bank(), Bank()], [Bank(), Bank()]]
            for toks in rows_(W["xattn_wo"], range(8), ys, 0, oxt, acc, True, True, (3, 1, 1, 3)):
                pass
            acc = (acc, toks)
            xuse[id(ys)] = [(PE.sem, PE.n)]

        if stop >= 7:
            xtok, xrs = norm(lambda t: X[:, t, :], gm, xs, None, acc, xt)
            acc = []
            act = {}

            def up(b, groups):
                s = Slot()
                box = act[b] = (s, [])

                def done(bk, toks):
                    for t in range(2):
                        v = s.v2[:, t, :]
                        a = AC(lambda e: e.activation(v, bk[t].v, ACT.Relu, scale=xrs[t][0]), toks[t], s.free, xrs[t][1])
                        bk[t].give(a)
                        box[1].append(PO(lambda e: e.tensor_tensor(v, v, v, ALU.mult), a))
                return cols(block(W["mlp_w1"], 512 * b), xs, xtok, done, groups, None if b else xtok)
            yt = {}
            yfree = [list(xuse[id(ys)]), list(xuse[id(ys)])]

            def turn_m(b, t):
                s, tk = act[b]
                bk = Bank()
                PE.wait([bk.free, tk[t]])
                for f in range(4):
                    p = PE(lambda e: e.transpose(bk.v[:, f * P:(f + 1) * P], s.v2[:, t, f * P:(f + 1) * P], ident))
                k0 = 4 * (b % 2)
                o = lambda l_: ys[:, l_, k0:k0 + 4, t * P:(t + 1) * P]
                a = AC(lambda e: e.copy(o(0), bk.g(4)), p, yfree[b % 2])
                d = DV(lambda e: e.tensor_tensor(o(1), bk.g(4), o(0).bitcast(F32), ALU.subtract), a)
                bk.give(d)
                if t == 1:
                    s.give(p)
                yt.setdefault(b, []).append(d)

            def down_m(b):
                last = b == 7
                for n, toks in enumerate(rows_(W["mlp_w2"], range(4 * b, 4 * b + 4), ys, 4 * (b % 2), yt[b], acc,
                                               b == 0, last, (1, 3) if last else None)):
                    if n in (1, 2) and not last:
                        turn_m(b + 1, n - 1)
                yfree[b % 2] = [toks[1]]
                return toks
            for b in range(8):
                if b == 1:
                    acc.extend([[Bank(), Bank()], [Bank(), Bank()]])
                    gf = get_gain("final")
                for k, _ in enumerate(up(b, (1, 1, 1, 1) if b else FIRST)):
                    if k in (1, 2) and b == 1:
                        turn_m(0, k - 1)
                if b:
                    down_m(b - 1)
            toks = down_m(7)
            for t in range(2):
                new = []
                for j in range(2):
                    v = X[:, t, j * 512:(j + 1) * 512]
                    new.append(DV(lambda e: e.tensor_tensor(v, acc[t][j].v, v, ALU.add), toks[t], xt[t]))
                xt[t] = new
            gi, gt = gf
            for t in range(2):
                s = Slot()
                ss = small(1)
                a = AC(lambda e: e.activation(s.v, X[:, t, :], ACT.Square, accum_out=ss), xt[t], s.free)
                r, rt = rsqrt(ss, 1, 1.0 / D, EPS, a)
                d = DV(lambda e: e.scalar_tensor_tensor(s.v, X[:, t, :], r, gi.v, ALU.mult, ALU.mult), rt, gt)
                SP.dma(lambda e: e.dma_start(out[0, t * P:(t + 1) * P, :], s.v), s_out, 16 * (t + 1), d)
            SP.wait([(s_out, 32)])
        else:
            done_early()
            SP.wait([(s_out, 16)] + [(s, 16) for s in s_ld[:ld[0]]])
        return order


def lay_out(inputs):
    a = {k: np.asarray(v) for k, v in inputs.items()}
    f = np.float32
    con, ret, dif = shape_constants()
    arr = {
        "x": a["x"], "mem": a["mem"], "mem2": a["mem_2"], "w_in": a["w_in"], "w_out": a["w_out"],
        "w_mem_kv": a["w_mem_kv"], "w_gate_up": a["w_gate_up"], "w_down": a["w_down"],
        "w_in_2": a["w_in_2"][0], "w_branch_gdn": a["w_branch_gdn_2"][0], "w_branch_gla": a["w_branch_gla_2"][0],
        "w_out_2": a["w_out_2"][0], "xattn_wq": a["xattn_wq_2"][0], "xattn_wk": a["xattn_wk_2"][0],
        "xattn_wv": a["xattn_wv_2"][0], "xattn_wo": a["xattn_wo_2"][0], "mlp_w1": a["mlp_w1_2"][0],
        "mlp_w2": a["mlp_w2_2"][0], "gate2": a["gla_w_gate2_2"][0],
        "con": con, "ret": ret, "dif": dif,
        "gains": np.stack([a["attn_norm_w"][0], a["attn_norm_w"][1], a["ffn_norm_w"][0], a["ffn_norm_w"][1],
                           a["mem_norm_w"], a["norm_mix_g_2"][0], a["norm_xattn_g_2"][0], a["norm_mem_g_2"][0],
                           a["norm_mlp_g_2"][0], a["norm_final_g_2"]]),
        "rows": np.concatenate([a["ret_gn_w"].reshape(-1), a["diff_subln_w"].reshape(-1),
                                a["gdn_norm_g_2"].reshape(-1), a["gla_norm_g_2"].reshape(-1),
                                a["gdn_a_log_2"].reshape(-1), a["gdn_dt_bias_2"].reshape(-1),
                                a["diff_lambda_q1"].reshape(-1), a["diff_lambda_k1"].reshape(-1),
                                a["diff_lambda_q2"].reshape(-1), a["diff_lambda_k2"].reshape(-1)])[None, :],
        "vecs": np.concatenate([
            a["gdn_conv_w_2"][0].reshape(4, 24, 128).transpose(2, 1, 0).reshape(128, 96),
            a["gla_b_gate_2"][0].reshape(4, 128).T,
            np.concatenate([a["diff_q_norm_w"][0]] * 2)[:, None], np.concatenate([a["diff_k_norm_w"][0]] * 2)[:, None],
            np.concatenate([a["mem_q_norm_w"]] * 2, axis=1).T, np.concatenate([a["mem_k_norm_w"]] * 2, axis=1).T], axis=1),
    }
    return {k: np.ascontiguousarray(v) for k, v in arr.items()}


def kernel(**inputs):
    import concourse.bacc as _bacc
    from concourse.bass_utils import run_bass_kernel_spmd as _run

    nc = _bacc.Bacc("TRN2", target_bir_lowering=False, num_devices=1)
    arr = lay_out(inputs)
    W = {k: nc.dram_tensor(f"in_{k}", v.shape, mybir.dt.from_np(v.dtype), kind="ExternalInput").ap()
         for k, v in arr.items()}
    out = nc.dram_tensor("out_0", (1, T, D), F32, kind="ExternalOutput").ap()
    scr = [nc.dram_tensor(f"kept_{i}", (P, 1024), F32, kind="Internal").ap() for i in range(4)]
    plan = build(nc, W, out, scr, None)
    build(nc, W, out, scr, plan)
    r = _run(nc, [{f"in_{k}": v for k, v in arr.items()}], core_ids=[0])
    return r.results[0]["out_0"]
```
